# Optimizing a Trainium2 kernel written in Bass

```python
import jax, jax.numpy as jnp
from jax import lax
import numpy as np

D_MODEL = 1024
BATCH = 1
SEQ = 2048
DEPTH = 1

CHUNK = 64
HEAD_DIM = 64
ROPE_THETA = 10000.0
EPS = 1e-6
MASK_VALUE = -1e30
BRANCH_W = D_MODEL // 2
N_BRANCH = 3
SWA_HEADS = BRANCH_W // HEAD_DIM
SWA_KV_HEADS = 2
SWA_WINDOW = 128
SWA_WIN_CHUNKS = SWA_WINDOW // CHUNK
DSA_HEADS = BRANCH_W // HEAD_DIM
IDX_HEADS = 4
IDX_DIM = 64
DSA_TOPK_MAX = 256
DSA_QBLOCK = 128
MEM_LEN = 256
MEM_HEADS = 4
MEM_HEAD_DIM = BRANCH_W // MEM_HEADS
A_Q = SWA_HEADS * HEAD_DIM
A_KV = SWA_KV_HEADS * HEAD_DIM
B_Q = DSA_HEADS * HEAD_DIM
B_KV = HEAD_DIM
B_QI = IDX_HEADS * IDX_DIM
B_KI = IDX_DIM
B_WI = IDX_HEADS
C_Q = MEM_HEADS * MEM_HEAD_DIM
GATE_COLS = N_BRANCH * D_MODEL
SPLIT_SIZES = (A_Q, A_KV, A_KV, BRANCH_W,
               B_Q, B_KV, B_KV, B_QI, B_KI, B_WI, BRANCH_W,
               C_Q, BRANCH_W,
               GATE_COLS)
IN_COLS = sum(SPLIT_SIZES)

kernel_name = "hybrid_swa_sink_dsa_memxattn_gated"

def _rmsnorm(x, g):
    xf = x.astype(jnp.float32)
    y = xf * lax.rsqrt(jnp.mean(xf * xf, axis=-1, keepdims=True) + EPS)
    return (y * g.astype(jnp.float32)).astype(x.dtype)

def _rope_tables(positions, dim, dtype):
    half = dim // 2
    inv = ROPE_THETA ** (-jnp.arange(half, dtype=jnp.float32) * 2.0 / dim)
    ang = positions.astype(jnp.float32)[..., None] * inv
    return (jnp.cos(ang).astype(dtype)[:, :, None, :],
            jnp.sin(ang).astype(dtype)[:, :, None, :])

def _rope(x, cos, sin):
    x1, x2 = jnp.split(x, 2, axis=-1)
    return jnp.concatenate([x1 * cos - x2 * sin, x2 * cos + x1 * sin], axis=-1)

def _split_points():
    pts, acc = [], 0
    for sz in SPLIT_SIZES[:-1]:
        acc += sz
        pts.append(acc)
    return pts

def _sliding_window_sink_attention(q, k, v, sinks):
    b, s, _, dh = q.shape
    nc = s // CHUNK
    g = SWA_HEADS // SWA_KV_HEADS
    qc = q.reshape(b, nc, CHUNK, SWA_KV_HEADS, g, dh)

    def band(t):
        t = t.reshape(b, nc, CHUNK, SWA_KV_HEADS, dh)
        tp = jnp.pad(t, ((0, 0), (SWA_WIN_CHUNKS - 1, 0), (0, 0), (0, 0), (0, 0)))
        return jnp.concatenate([tp[:, j:j + nc] for j in range(SWA_WIN_CHUNKS)], axis=2)

    kb, vb = band(k), band(v)
    key_chunk = (jnp.arange(nc)[:, None] - (SWA_WIN_CHUNKS - 1)
                 + jnp.arange(SWA_WIN_CHUNKS * CHUNK)[None, :] // CHUNK)
    valid = key_chunk >= 0
    scores = jnp.einsum('bnqkgd,bnskd->bnkgqs', qc, kb).astype(jnp.float32) * (dh ** -0.5)
    scores = jnp.where(valid[None, :, None, None, None, :], scores, MASK_VALUE)
    sink = jnp.broadcast_to(sinks.astype(jnp.float32).reshape(1, 1, SWA_KV_HEADS, g, 1, 1),
                            scores.shape[:-1] + (1,))
    p = jax.nn.softmax(jnp.concatenate([scores, sink], axis=-1), axis=-1)[..., :-1]
    o = jnp.einsum('bnkgqs,bnskd->bnqkgd', p.astype(v.dtype), vb)
    return o.reshape(b, s, SWA_HEADS * dh)

def _dsa_sparse_attention(q, k, v, q_idx, k_idx, w_idx):
    b, s, _, dh = q.shape
    topk = min(DSA_TOPK_MAX, s // 4)
    nqb = s // DSA_QBLOCK

    def blocks(t):
        return jnp.swapaxes(t.reshape((b, nqb, DSA_QBLOCK) + t.shape[2:]), 0, 1)

    tpos = jnp.arange(s, dtype=jnp.int32).reshape(nqb, DSA_QBLOCK)
    key_pos = jnp.arange(s, dtype=jnp.int32)
    w_scaled = w_idx.astype(jnp.float32) * ((IDX_HEADS ** -0.5) * (IDX_DIM ** -0.5))
    gather = jax.vmap(lambda table, idx: table[idx])

    def one_block(args):
        qb, qib, wb, tp = args
        logits = jnp.einsum('bqhd,bsd->bqhs', qib, k_idx).astype(jnp.float32)
        score = jnp.einsum('bqhs,bqh->bqs', jax.nn.relu(logits), wb)
        limit = (tp // CHUNK + 1) * CHUNK
        admissible = key_pos[None, :] < limit[:, None]
        score = jnp.where(admissible[None], score, -jnp.inf)
        _, sel = lax.top_k(score, topk)
        valid = sel < limit[None, :, None]
        kg = gather(k, sel)
        vg = gather(v, sel)
        sc = jnp.einsum('bqhd,bqkd->bhqk', qb, kg).astype(jnp.float32) * (dh ** -0.5)
        sc = jnp.where(valid[:, None], sc, MASK_VALUE)
        p = jax.nn.softmax(sc, axis=-1).astype(vg.dtype)
        return jnp.einsum('bhqk,bqkd->bqhd', p, vg)

    o = lax.map(one_block, (blocks(q), blocks(q_idx), blocks(w_scaled), tpos))
    return jnp.swapaxes(o, 0, 1).reshape(b, s, DSA_HEADS * dh)

def _memory_cross_attention(q, k, v):
    dc = q.shape[-1]
    sc = jnp.einsum('bshd,bmhd->bhsm', q, k).astype(jnp.float32) * (dc ** -0.5)
    p = jax.nn.softmax(sc, axis=-1).astype(v.dtype)
    o = jnp.einsum('bhsm,bmhd->bshd', p, v)
    return o.reshape(q.shape[0], q.shape[1], MEM_HEADS * dc)

def _hybrid_layer(x, mem, cos, sin, g_in, w_in, attn_sinks, g_mem, w_mem_kv, w_branch, w_out):
    b, s, _ = x.shape
    h = _rmsnorm(x, g_in)
    proj = h @ w_in
    (a_q, a_k, a_v, a_z, b_q, b_k, b_v, b_qi, b_ki, b_wi, b_z,
     c_q, c_z, gates) = jnp.split(proj, _split_points(), axis=-1)

    a_q = _rope(a_q.reshape(b, s, SWA_HEADS, HEAD_DIM), cos, sin)
    a_k = _rope(a_k.reshape(b, s, SWA_KV_HEADS, HEAD_DIM), cos, sin)
    a_v = a_v.reshape(b, s, SWA_KV_HEADS, HEAD_DIM)
    y_a = _sliding_window_sink_attention(a_q, a_k, a_v, attn_sinks)

    b_q = _rope(b_q.reshape(b, s, DSA_HEADS, HEAD_DIM), cos, sin)
    b_k = _rope(b_k[:, :, None, :], cos, sin)[:, :, 0]
    b_qi = _rope(b_qi.reshape(b, s, IDX_HEADS, IDX_DIM), cos, sin)
    b_ki = _rope(b_ki[:, :, None, :], cos, sin)[:, :, 0]
    y_b = _dsa_sparse_attention(b_q, b_k, b_v, b_qi, b_ki, b_wi)

    m_n = _rmsnorm(mem, g_mem)
    m_k, m_v = jnp.split(m_n @ w_mem_kv, 2, axis=-1)
    m_k = m_k.reshape(b, -1, MEM_HEADS, MEM_HEAD_DIM)
    m_v = m_v.reshape(b, -1, MEM_HEADS, MEM_HEAD_DIM)
    y_c = _memory_cross_attention(c_q.reshape(b, s, MEM_HEADS, MEM_HEAD_DIM), m_k, m_v)

    ys = jnp.stack([y_a * jax.nn.silu(a_z), y_b * jax.nn.silu(b_z), y_c * jax.nn.silu(c_z)], axis=2)
    u = jnp.einsum('bsnc,ncd->bsnd', ys, w_branch)
    merged = jnp.sum(jax.nn.sigmoid(gates.reshape(b, s, N_BRANCH, D_MODEL)) * u, axis=2)
    return x + merged @ w_out

def setup_inputs(seed: int = 0) -> dict:
    key = jax.random.key(seed)
    ks = jax.random.split(key, 12)
    x = jax.random.normal(ks[0], (BATCH, SEQ, D_MODEL), jnp.float32)
    mem = jax.random.normal(ks[1], (BATCH, MEM_LEN, D_MODEL), jnp.float32)
    offsets = jax.random.randint(ks[2], (BATCH, 1), 0, 16, dtype=jnp.int32) * CHUNK
    positions = (jnp.arange(SEQ, dtype=jnp.int32)[None, :] + offsets).astype(jnp.int32)
    g_in = 1.0 + 0.02 * jax.random.normal(ks[3], (DEPTH, D_MODEL), jnp.float32)
    w_in = jax.random.normal(ks[4], (DEPTH, D_MODEL, IN_COLS), jnp.float32) * D_MODEL ** -0.5
    attn_sinks = 0.5 * jax.random.normal(ks[5], (DEPTH, SWA_HEADS), jnp.float32)
    g_mem = 1.0 + 0.02 * jax.random.normal(ks[6], (DEPTH, D_MODEL), jnp.float32)
    w_mem_kv = jax.random.normal(ks[7], (DEPTH, D_MODEL, 2 * BRANCH_W), jnp.float32) * D_MODEL ** -0.5
    w_branch = jax.random.normal(ks[8], (DEPTH, N_BRANCH, BRANCH_W, D_MODEL), jnp.float32) * BRANCH_W ** -0.5
    w_out = jax.random.normal(ks[9], (DEPTH, D_MODEL, D_MODEL), jnp.float32) * D_MODEL ** -0.5
    g_final = 1.0 + 0.02 * jax.random.normal(ks[10], (D_MODEL,), jnp.float32)
    return {'x': x, 'mem': mem, 'positions': positions, 'g_in': g_in, 'w_in': w_in,
            'attn_sinks': attn_sinks, 'g_mem': g_mem, 'w_mem_kv': w_mem_kv,
            'w_branch': w_branch, 'w_out': w_out, 'g_final': g_final}

def reference(x, mem, positions, g_in, w_in, attn_sinks, g_mem, w_mem_kv, w_branch, w_out, g_final):
    cos, sin = _rope_tables(positions, HEAD_DIM, x.dtype)
    for l in range(DEPTH):
        x = _hybrid_layer(x, mem, cos, sin, g_in[l], w_in[l], attn_sinks[l], g_mem[l],
                          w_mem_kv[l], w_branch[l], w_out[l])
    return _rmsnorm(x, g_final)


_drawn_inputs = setup_inputs


def setup_inputs(seed=0):
    import zlib

    import numpy as np

    out = dict(_drawn_inputs(seed))
    spreads = {}
    factors = {'g_in': 8.0, 'attn_sinks': 8.0, 'g_mem': 8.0, 'g_final': 2.922}
    for name, (base, spread) in spreads.items():
        noise = np.random.default_rng([zlib.crc32(name.encode()), seed]).standard_normal(out[name].shape)
        drawn = base * np.exp(spread * noise) if base else spread * noise
        out[name] = __import__('jax').numpy.asarray(drawn.astype(out[name].dtype))
    for name, factor in factors.items():
        out[name] = (out[name] * factor).astype(out[name].dtype)
    return out
```

```python
from contextlib import ExitStack

import numpy as np
import concourse.bass as bass
from concourse import mybir

F32, F32R, I32 = mybir.dt.float32, mybir.dt.float32r, mybir.dt.int32
ALU = mybir.AluOpType
ACT = mybir.ActivationFunctionType
AX = mybir.AxisListType

P = 128
D, SEQ, MEM = 1024, 2048, 256
KC = D // P
BW = D // 2
BC = BW // P
T = 512
NG = SEQ // T
NT = T // P
CHUNK, HD = 64, 64
TOPK = 256
EPS = 1e-6
THETA = 10000.0
MASKED = -1e30
LOWEST = -3.4028234663852886e38

A_Q, A_K, A_V, A_Z = 0, 512, 640, 768
B_Q, B_KV, B_QI, B_KIW, B_Z = 1280, 1792, 1920, 2176, 2244
C_Q, C_Z, GATES = 2756, 3268, 3780


class Step:

    def __init__(self, kind, role=None, source=None, src=None, which=None, branch=None, g=None, i=None,
                 h=None, m=None, tt=None, of=None, col=None, kc=None, width=None, moving=None, n_tok=None,
                 first=None, keys=None, chunks=None, groups=None, items=None, parts=None, unit=None,
                 wt=None, u=None, evac=None, used=None, f=None, x=None, y=None, k=None, a=None, tr=None,
                 p=None, before=None, turn_r=None):
        self.kind = kind
        self.role, self.source, self.src, self.which, self.branch, self.g = role, source, src, which, branch, g
        self.i, self.h, self.m, self.tt, self.of, self.col = i, h, m, tt, of, col
        self.kc, self.width, self.moving, self.n_tok, self.first, self.keys = kc, width, moving, n_tok, first, keys
        self.chunks, self.groups, self.items, self.parts, self.unit, self.wt = chunks, groups, items, parts, unit, wt
        self.u, self.evac, self.used, self.f, self.x, self.y = u, evac, used, f, x, y
        self.k, self.a, self.tr, self.p, self.before, self.turn_r = k, a, tr, p, before, turn_r


def order_of_work():
    steps = []
    n = dict(wt=0, u=0, tr=0, s=0, f=0, x=0, k=0, a=0, y=0, rel=0, p=0, stacked=0)
    count = dict(act_pj=0, dve_pj=0, act_s=0, dve_s=0)
    pj_freed, s_freed = [], []

    def take(name, k=1):
        n[name] += k
        return n[name] - k

    def freed(ring, engine, of):
        count[f"{engine}_{of}"] += 1
        ring.append((engine, count[f"{engine}_{of}"]))

    def unit(role, src, col, kc=KC, width=P, moving="h", n_tok=T, **more):
        st = Step("unit", role=role, src=src, col=col, kc=kc, width=width, moving=moving,
                  n_tok=n_tok, wt=take("wt"), u=take("u"), **more)
        freed(pj_freed, "act", "pj")
        st.evac = pj_freed[-1][1]
        if role in ("kv", "qi", "kiw", "q", "ak", "av", "mv"):
            st.f = take("f")
        if role in ("z", "mk", "cq", "gate"):
            st.x = take("x")
        if role == "up":
            st.x = n["x"] - 1
        steps.append(st)
        return st

    def turned(specs):
        units = []
        for k in range(len(specs) + 2):
            if k < len(specs):
                role, src, col, more = specs[k]
                units.append(unit(role, src, col, **more))
            if k >= 2:
                st = units[k - 2]
                banks = {"kv": 2, "qi": 4, "kiw": 1, "q": 2, "ak": 4}.get(st.role, 0)
                if banks:
                    steps.append(Step("restack", unit=st, tr=take("tr", banks), k=st.k, before=n["stacked"]))
                    n["stacked"] = n["tr"]
            if 1 <= k <= len(specs):
                st = units[k - 1]
                if st.role not in ("av", "mv"):
                    st.k = take("k")
                steps.append(Step("turn", unit=st, tr=take("tr")))
                st.turn_r = steps[-1].tr

    def norm(source, g):
        steps.append(Step("norm", source=source, g=g, tr=take("tr", KC)))

    def attention(branch, g):
        if branch == "b":
            items, keys = [(tt, h) for tt in range(NT) for h in range(8)], T * (g + 1)
            chunks = [(c, min(1024, keys - c)) for c in range(0, keys, 1024)]
        else:
            items, keys = [(None, h) for h in range(4 if branch == "c" else 8)], 256
            chunks = [(0, NT * 256)]
        group = Step("attention", branch=branch, g=g, keys=keys, items=[])
        for tt, h in items:
            it = Step("item", tt=tt, h=h, a=take("a"), u=take("u"), chunks=[])
            freed(pj_freed, "dve", "pj")
            it.used = pj_freed[-1][1]
            for c, size in chunks:
                it.chunks.append((c, size, take("s")))
                freed(s_freed, "dve", "s")
            it.groups = keys // T if branch == "b" else 2
            it.tr, it.p = take("tr", it.groups), take("p", it.groups)
            group.items.append(it)
        group.x = n["x"]
        steps.append(group)

    def branch(which, g):
        steps.append(Step("split_y", y=take("y"), used=count["dve_pj"]))
        for m in range(KC):
            unit("gate", "w_in", GATES + which * D + m * P, m=m)
            unit("up", "w_branch", m * P, kc=BC, moving="y", m=m, which=which, y=n["y"],
                 first=(which == 2), g=g)

    norm("mem", 0)
    for h in range(4):
        unit("mk", "w_mem_kv", h * P, n_tok=MEM, h=h)
    turned([("mv", "w_mem_kv", BW + h * P, dict(n_tok=MEM, h=h)) for h in range(4)])
    steps.append(Step("save_mem", x=n["x"], tr=n["tr"]))
    for g in range(NG):
        norm("x", g)
        turned([("kv", "w_in", B_KV, dict(g=g)),
                ("qi", "w_in", B_QI, dict(g=g, i=0)),
                ("qi", "w_in", B_QI + P, dict(g=g, i=1)),
                ("kiw", "w_in", B_KIW, dict(g=g, width=HD + 4))])
        st = Step("index", g=g, keys=T * (g + 1), parts=[], tr=n["tr"])
        for tt in range(NT):
            for h in range(4):
                for c in range(0, st.keys, 1024):
                    st.parts.append((tt, h, c, min(1024, st.keys - c), take("s"), take("rel")))
                    freed(s_freed, "act", "s")
        steps.append(st)
        for i in range(4):
            unit("z", "w_in", C_Z + i * P, i=i, g=g, y=n["y"])
        for i in range(4):
            unit("cq", "w_in", C_Q + i * P, i=i)
        attention("c", g)
        branch(2, g)
        for i in range(4):
            unit("z", "w_in", A_Z + i * P, i=i, g=g, y=n["y"])
        turned([("ak", "w_in", A_K, dict(g=g)), ("av", "w_in", A_V, dict(g=g))]
               + [("q", "w_in", A_Q + i * P, dict(g=g, i=i, of="a")) for i in range(4)])
        attention("a", g)
        branch(0, g)
        steps.append(Step("select", g=g, keys=T * (g + 1)))
        for i in range(4):
            unit("z", "w_in", B_Z + i * P, i=i, g=g, y=n["y"])
        turned([("q", "w_in", B_Q + i * P, dict(g=g, i=i, of="b")) for i in range(4)])
        attention("b", g)
        branch(1, g)
        steps.append(Step("split_m", g=g, x=n["x"]))
        for m in range(KC):
            unit("out", "w_out", m * P, moving="m", m=m, g=g)
        steps.append(Step("finish", g=g, tr=take("tr", 2 * NT), used=count["dve_pj"], y=n["y"],
                          evac=count["act_pj"]))
    return steps, pj_freed, s_freed, n


def hybrid_block(nc, x, mem, positions, g_in, w_in, attn_sinks, g_mem, w_mem_kv, w_branch, w_out,
                 g_final, out):
    steps, pj_freed, s_freed, total = order_of_work()
    x_v = x[0].rearrange("(g t p) d -> g p t d", t=NT, p=P)
    out_v = out[0].rearrange("(g t p) d -> g p t d", t=NT, p=P)
    mem_v = mem[0].rearrange("(t p) d -> p t d", p=P)
    weights = {"w_in": w_in[0].rearrange("(k p) n -> p k n", p=P),
               "w_mem_kv": w_mem_kv[0].rearrange("(k p) n -> p k n", p=P),
               "w_out": w_out[0].rearrange("(k p) n -> p k n", p=P)}
    up_v = w_branch[0].rearrange("b (k p) n -> b p k n", p=P)
    mem_scratch = nc.dram_tensor("mem_scratch", (P, 4096), F32, kind="Internal").ap()

    ctx = ExitStack()
    with ctx:
        at = [(nc.sbuf_base + 63) // 64 * 64]

        def sb(name, shape, dt=F32, offset=None):
            size = int(np.prod(shape[1:])) * 4
            if offset is None:
                offset, at[0] = at[0], at[0] + (size + 31) // 32 * 32
            return nc.alloc_sbuf_tensor_at(name, shape, dt, offset=offset)

        def region(size):
            at[0] += size
            return at[0] - size

        def sem(name):
            return ctx.enter_context(nc.semaphore(name))

        hH, hL = sb("hH", [P, KC, T], F32R), sb("hL", [P, KC, T], F32R)
        raw, wH, wL = (sb(n, [P, 2, KC, P], d) for n, d in (("raw", F32), ("wH", F32R), ("wL", F32R)))
        kA, kB, kiS = (sb(n, [P, SEQ], F32R) for n in ("kA", "kB", "kiS"))
        vS = sb("vS", [P, HD + SEQ // P * P], F32R)
        wkA, wkB = sb("wkA", [P, 2, P + T], F32R), sb("wkB", [P, 2, P + T], F32R)
        wv = sb("wv", [P, HD + (NT + 1) * 2 * P], F32R)
        score = sb("score", [P, NT, SEQ])
        merged_at = region(16384)
        merged = sb("merged", [P, KC, T], offset=merged_at)
        ob = sb("ob", [P, KC, T], offset=merged_at)
        memkv = sb("memkv", [P, 4096], F32R, offset=merged_at)
        ysH, ysL = sb("ysH", [P, BC, T], F32R), sb("ysL", [P, BC, T], F32R)
        zs_at = region(8192)
        zs = sb("zs", [P, BC, T], offset=zs_at)
        gfin = sb("gfin", [P, D], offset=zs_at)
        qst_at = region(16384)
        qst = sb("qst", [P, 8, T], F32R, offset=qst_at)
        junk = sb("junk", [P, D], offset=qst_at)
        p_at = region(16384)
        prob = sb("prob", [P, 2, SEQ], offset=p_at)
        xs = sb("xs", [P, NT, D], offset=p_at)
        fT = sb("fT", [P, 2, T], offset=p_at)
        t1 = sb("t1", [P, T], offset=p_at + 4096)
        t2 = sb("t2", [P, T], offset=p_at + 6144)
        stack = sb("stack", [P, 2, 1024], F32R, offset=p_at + 8192)
        rel = sb("rel", [P, 2, 1024], offset=p_at + 8192)
        pt_at = region(8192)
        ptH = sb("ptH", [P, 2, T], F32R, offset=pt_at)
        ptL = sb("ptL", [P, 2, T], F32R, offset=pt_at + 4096)
        sg = sb("sg", [P, 2, T], offset=pt_at)
        ub = sb("ub", [P, 2, T], offset=pt_at + 4096)
        ident = sb("ident", [P, P])
        cos, sin = sb("cos", [P, NT, 32]), sb("sin", [P, NT, 32])
        wmask = sb("wmask", [P, 2, 256])
        wi = sb("wi", [P, NT, 4])
        inv = sb("inv", [P, 32])
        posi, posf = sb("posi", [P, SEQ // P], I32), sb("posf", [P, SEQ // P])
        gcol = sb("gcol", [P, 2, KC])
        sink, sink8 = sb("sink", [P, 8]), sb("sink8", [P, 8])
        small = sb("small", [P, 9, NT])
        ssq, var, rstd, tmp, top, den, rden, cnt, need = (small[:, i, :] for i in range(9))
        snk, esnk, nmx, psum = (sb(n, [P, 2, NT]) for n in ("snk", "esnk", "nmx", "psum"))
        bits = sb("bits", [P, 5, NT], I32)
        ubits, cand, flip, thr, gi = (bits[:, i, :] for i in range(5))
        assert at[0] <= nc.sbuf_usable_end, at[0]
        ang, turns, folded = (score[:, 0, i * 128:(i + 1) * 128].rearrange("p (t j) -> p t j", t=NT) for i in range(3))

        def t1_heads(nh):
            return t1[:, 0:NT * nh * HD].rearrange("p (n c) -> p n c", c=HD)

        def stack_view(which, nh):
            return stack[:, which, 0:NT * nh * P].rearrange("p (n a c) -> p n a c", a=2, c=HD)

        def twice(ap, n):
            return ap.unsqueeze(2).broadcast_to([P, n, 2, HD])

        def tabled(table, n):
            return table[:, :, :].unsqueeze(2).broadcast_to([P, NT, n, 32])
        mKH = memkv[:, 0:1024].rearrange("p (h m) -> p h m", h=4)
        mKL = memkv[:, 1024:2048].rearrange("p (h m) -> p h m", h=4)
        mVH = memkv[:, 2048:3072].rearrange("p (t n) -> p t n", t=2)
        mVL = memkv[:, 3072:4096].rearrange("p (t n) -> p t n", t=2)

        PJ = [ctx.enter_context(nc.psum_tensor(f"PJ{i}", [P, T], F32)) for i in range(2)]
        TR = [ctx.enter_context(nc.psum_tensor(f"TR{i}", [P, T], F32)) for i in range(2)]
        SC = [ctx.enter_context(nc.psum_tensor(f"SC{i}", [P, 1024], F32)) for i in range(2)]

        names = """x_in pos_in small_in gfin_in raw_in0 raw_in1 mem_out mem_in store
            hi_ready lo_ready tile_done act_pj dve_pj y_done tr_full tr_free s_full act_s dve_s
            pv_done stack_hi stack_lo roped rel_used mixed y_hi y_lo m_hi m_lo p_sub p_exp p_ready
            pt_hi h_hi squared var_ready rooted scaled selected out_ready consts dve_step pool_step
            act_step tables_in sin_ready ang_ready""".split()
        S = {n: sem(n) for n in names}
        raw_in = [S["raw_in0"], S["raw_in1"]]
        block = ctx.enter_context(nc.Block())
        freed_by = {"act_pj": S["act_pj"], "dve_pj": S["dve_pj"], "act_s": S["act_s"], "dve_s": S["dve_s"]}

        units = [st for st in steps if st.kind == "unit"]
        norms = [st for st in steps if st.kind == "norm"]

        def wait_bank(eng, ring, index, of):
            if index >= 2:
                engine, value = ring[index - 2]
                eng.wait_ge(freed_by[f"{engine}_{of}"], value)

        @block.sync
        def _(sp):
            def load_tile(wt):
                if wt >= 2:
                    sp.wait_ge(S["lo_ready"], wt - 1)
                st = units[wt]
                src = up_v[st.which] if st.src == "w_branch" else weights[st.src]
                sp.dma_start(raw[:, wt % 2, 0:st.kc, 0:st.width],
                             src[:, :, st.col:st.col + st.width]).then_inc(raw_in[wt % 2], 16)

            sp.dma_start(xs[:, 0:2, :], mem_v).then_inc(S["x_in"], 16)
            sp.dma_start(posi[:, :], positions).then_inc(S["small_in"], 16)
            sp.dma_start(gcol[:, 0, :], g_mem).then_inc(S["small_in"], 16)
            sp.dma_start(gcol[:, 1, :], g_in).then_inc(S["small_in"], 16)
            sp.dma_start(sink[:, :], attn_sinks.broadcast_to([P, 8])).then_inc(S["small_in"], 16)
            load_tile(0)
            load_tile(1)
            loads = 1
            for st in steps:
                if st.kind == "norm" and st.source == "x":
                    if st.g:
                        sp.wait_ge(S["store"], 16 * st.g)
                    else:
                        sp.wait_ge(S["mem_out"], 16)
                    sp.dma_start(xs[:, :, :], x_v[st.g]).then_inc(S["x_in"], 16)
                elif st.kind == "save_mem":
                    sp.wait_ge(S["mixed"], st.x)
                    sp.wait_ge(S["tr_free"], st.tr)
                    sp.dma_start(mem_scratch, memkv[:, :].bitcast(F32)).then_inc(S["mem_out"], 16)
                elif st.kind == "unit":
                    if st.wt + 2 < len(units):
                        load_tile(st.wt + 2)
                elif st.kind == "finish":
                    sp.wait_ge(S["dve_pj"], st.used)
                    sp.dma_start(xs[:, :, :], x_v[st.g]).then_inc(S["x_in"], 16)
                    sp.wait_ge(S["y_lo"], st.y)
                    sp.dma_start(gfin[:, :], g_final.unsqueeze(0).broadcast_to([P, D])).then_inc(S["gfin_in"], 16)
                    sp.wait_ge(S["out_ready"], st.g + 1)
                    sp.dma_start(out_v[st.g], xs[:, :, :]).then_inc(S["store"], 16)
                    if st.g + 1 < NG:
                        sp.wait_ge(S["tr_free"], st.tr + 2 * NT)
                        sp.dma_start(memkv[:, :].bitcast(F32), mem_scratch).then_inc(S["mem_in"], 16)
            sp.wait_ge(S["store"], 16 * NG)

        @block.tensor
        def _(pe):
            def transposes(tr, blocks):
                if tr >= 2:
                    pe.wait_ge(S["tr_free"], tr - 1)
                for at_col, src in blocks:
                    k, m = src.shape[0], src.shape[1]
                    last = nc.tensor.transpose(TR[tr % 2][0:m, at_col:at_col + k], src, ident[0:k, 0:k])
                last.then_inc(S["tr_full"], 1)

            def scores(it, branch):
                for c, size, s in it.chunks:
                    wait_bank(pe, s_freed, s, "s")
                    bank = SC[s % 2]
                    if branch == "b":
                        lhs = qst[:, it.h, it.tt * P:(it.tt + 1) * P]
                        for o in range(0, size, 512):
                            nc.tensor.matmul(bank[:, o:o + 512], lhs, kA[:, c + o:c + o + 512], start=True, stop=False)
                            last = nc.tensor.matmul(bank[:, o:o + 512], lhs, kB[:, c + o:c + o + 512], start=False, stop=True)
                    for tt in range(NT):
                        o = tt * 256
                        tok = slice(tt * P, (tt + 1) * P)
                        if branch == "a":
                            lhs, kv = qst[:, it.h, tok], it.h // 4
                            keys = slice(tt * P, tt * P + 256)
                            nc.tensor.matmul(bank[:, o:o + 256], lhs, wkA[:, kv, keys], start=True, stop=False)
                            last = nc.tensor.matmul(bank[:, o:o + 256], lhs, wkB[:, kv, keys], start=False, stop=True)
                        elif branch == "c":
                            qh, ql = qst[:, it.h, tok], qst[:, 4 + it.h, tok]
                            nc.tensor.matmul(bank[:, o:o + 256], qh, mKH[:, it.h, :], start=True, stop=False)
                            nc.tensor.matmul(bank[:, o:o + 256], qh, mKL[:, it.h, :], start=False, stop=False)
                            last = nc.tensor.matmul(bank[:, o:o + 256], ql, mKH[:, it.h, :], start=False, stop=True)
                    last.then_inc(S["s_full"], 1)

            def values(it, branch):
                slot = prob[:, it.a % 2, :]
                pe.wait_ge(S["p_ready"], it.a + 1)
                for j in range(it.groups + 1):
                    if j < it.groups:
                        if branch == "b":
                            cols = [(4 * j + i) * P for i in range(4)]
                        else:
                            cols = [tt * 256 + j * P for tt in range(NT)]
                        transposes(it.tr + j, [(i * P, slot[:, c:c + P]) for i, c in enumerate(cols)])
                    if j >= 1:
                        products(it, branch, j - 1)

            def products(it, branch, j):
                if j == 0:
                    wait_bank(pe, pj_freed, it.u, "pj")
                pe.wait_ge(S["tr_free"], it.tr + j + 1)
                H, L = ptH[:, (it.p + j) % 2, :], ptL[:, (it.p + j) % 2, :]
                bank, odd = PJ[it.u % 2], it.h % 2
                rows = P if odd or branch == "c" else HD
                end = j == it.groups - 1
                if branch == "c":
                    vh, vl = mVH[:, j, it.h * P:(it.h + 1) * P], mVL[:, j, it.h * P:(it.h + 1) * P]
                    for i, (v, p) in enumerate(((vh, H), (vl, H), (vh, L))):
                        last = nc.tensor.matmul(bank[:, :], v, p, start=(j == 0 and i == 0), stop=(end and i == 2))
                else:
                    for b in range(4):
                        if branch == "b":
                            src, base, col = vS, (4 * j + b) * P, 0
                        else:
                            src, base, col = wv, ((b + j) * 2 + it.h // 4) * P, b * P
                        vh = src[:, base:base + P] if odd else src[:, HD + base:2 * HD + base]
                        vl = src[:, HD + base:HD + base + P] if odd else src[:, 2 * HD + base:3 * HD + base]
                        p = slice(b * P, (b + 1) * P)
                        for i, (v, pr) in enumerate(((vh, H), (vl, H), (vh, L))):
                            last = nc.tensor.matmul(bank[0:rows, col:col + P], v, pr[:, p],
                                                    start=(j == 0 and b == 0 and i == 0),
                                                    stop=(end and i == 2 and (branch == "a" or b == 3)),
                                                    skip_group_check=True)
                last.then_inc(S["pv_done"], 1)

            pe.wait_ge(S["consts"], 1)
            for st in steps:
                if st.kind == "norm":
                    nt = 2 if st.source == "mem" else NT
                    pe.wait_ge(S["scaled"], norms.index(st) + 1)
                    for k in range(KC):
                        transposes(st.tr + k, [(t * P, xs[:, t, k * P:(k + 1) * P]) for t in range(nt)])
                    pe.wait_ge(S["tr_free"], st.tr + KC)
                elif st.kind == "unit":
                    pe.wait_ge(S["lo_ready"], st.wt + 1)
                    wait_bank(pe, pj_freed, st.u, "pj")
                    if st.moving == "y":
                        pe.wait_ge(S["y_lo"], st.y)
                    if st.moving == "m":
                        pe.wait_ge(S["m_lo"], st.g + 1)
                    mH, mL = (ysH, ysL) if st.moving == "y" else (hH, hL)
                    o = PJ[st.u % 2][0:st.width, 0:st.n_tok]
                    b = st.wt % 2
                    for k in range(st.kc):
                        for i, (lhs, rhs) in enumerate(((wH, mH), (wH, mL), (wL, mH))):
                            last = nc.tensor.matmul(o, lhs[:, b, k, 0:st.width], rhs[:, k, 0:st.n_tok],
                                                    start=(k == 0 and i == 0), stop=(k == st.kc - 1 and i == 2))
                    last.then_inc(S["tile_done"], 1)
                elif st.kind == "turn":
                    un = st.unit
                    pe.wait_ge(S["act_pj"], un.evac)
                    src = fT[:, un.f % 2, :]
                    transposes(st.tr, [(t * P, src[0:un.width, t * P:(t + 1) * P]) for t in range(un.n_tok // P)])
                elif st.kind == "restack":
                    un = st.unit
                    pe.wait_ge(S["stack_lo"], st.k + 1)
                    nh = {"kv": 1, "kiw": 1}.get(un.role, 2)
                    for j in range({"kv": 2, "qi": 4, "kiw": 1, "q": 2, "ak": 4}[un.role]):
                        which, h = divmod(j, nh)
                        transposes(st.tr + j, [(t * P, stack[:, which, (t * nh + h) * P:(t * nh + h + 1) * P].bitcast(F32))
                                              for t in range(NT)])
                elif st.kind == "index":
                    pe.wait_ge(S["tr_free"], st.tr)
                    for tt, h, c, size, s, _ in st.parts:
                        wait_bank(pe, s_freed, s, "s")
                        for o in range(0, size, 512):
                            for i in range(2):
                                last = nc.tensor.matmul(SC[s % 2][:, o:o + 512], qst[:, 4 * i + h, tt * P:(tt + 1) * P],
                                                        kiS[:, c + o:c + o + 512], start=(i == 0), stop=(i == 1))
                        last.then_inc(S["s_full"], 1)
                elif st.kind == "attention":
                    if st.branch == "c":
                        pe.wait_ge(S["mixed"], st.x)
                        if st.g:
                            pe.wait_ge(S["mem_in"], 16 * st.g)
                    else:
                        pe.wait_ge(S["tr_free"], st.items[0].tr)
                    scores(st.items[0], st.branch)
                    for i, it in enumerate(st.items):
                        if i + 1 < len(st.items):
                            scores(st.items[i + 1], st.branch)
                        values(it, st.branch)
                elif st.kind == "finish":
                    pe.wait_ge(S["act_pj"], st.evac)
                    for j in range(2 * NT):
                        tt, half = divmod(j, 2)
                        transposes(st.tr + j, [(m * P, ob[:, 4 * half + m, tt * P:(tt + 1) * P]) for m in range(4)])

        @block.scalar
        def _(act):
            def split_hi(wt):
                un = units[wt]
                act.wait_ge(raw_in[wt % 2], 16 * (wt // 2 + 1))
                if wt >= 2:
                    act.wait_ge(S["tile_done"], wt - 1)
                nc.scalar.activation(wH[:, wt % 2, 0:un.kc, 0:un.width], raw[:, wt % 2, 0:un.kc, 0:un.width],
                                     ACT.Copy).then_inc(S["hi_ready"], 1)

            n_squares = [0]

            def squares(tiles):
                for t in range(tiles):
                    if n_squares[0]:
                        act.wait_ge(S["squared"], n_squares[0])
                    n_squares[0] += 1
                    nc.scalar.activation(junk[:, :], xs[:, t, :], ACT.Square,
                                         accum_out=ssq[:, t:t + 1]).then_inc(S["squared"], 1)

            def root(n, tiles):
                act.wait_ge(S["var_ready"], n)
                nc.scalar.activation(rstd[:, 0:tiles], var[:, 0:tiles], ACT.Sqrt).then_inc(S["rooted"], 1)

            def exps(it, branch, keys):
                act.wait_ge(S["p_sub"], it.a + 1)
                scale = (P if branch == "c" else HD) ** -0.5
                slot = prob[:, it.a % 2, :]
                if branch == "b":
                    nc.scalar.activation(slot[:, 0:keys], slot[:, 0:keys], ACT.Exp, bias=nmx[:, it.a % 2, 0:1],
                                         scale=scale, accum_out=psum[:, it.a % 2, 0:1]).then_inc(S["p_exp"], 1)
                else:
                    if branch == "a":
                        nc.scalar.activation(esnk[:, it.a % 2, :], snk[:, it.a % 2, :], ACT.Exp, scale=scale)
                    nc.scalar.activation(slot[:, 0:1024], slot[:, 0:1024], ACT.Exp, scale=scale).then_inc(S["p_exp"], 1)

            def turned_hi(it):
                for j in range(it.groups):
                    tr, p = it.tr + j, it.p + j
                    act.wait_ge(S["tr_full"], tr + 1)
                    if p >= 2:
                        act.wait_ge(S["pv_done"], p - 1)
                    nc.scalar.activation(ptH[:, p % 2, :], TR[tr % 2][:, :], ACT.Copy).then_inc(S["pt_hi"], 1)

            turn_r = []
            mixes_before = {}
            n_norm = n_root = 0
            split_hi(0)
            split_hi(1)
            for st in steps:
                if st.kind == "norm":
                    n, nt = norms.index(st), 2 if st.source == "mem" else NT
                    if st.g == 0:
                        act.wait_ge(S["small_in"], 64)
                    act.wait_ge(S["x_in"], 16 * (1 if st.source == "mem" else 2 + 2 * st.g))
                    if st.g:
                        act.wait_ge(S["out_ready"], st.g)
                    squares(nt)
                    n_root += 1
                    root(n_root, nt)
                    if st.source == "x":
                        for i, table in enumerate((sin, cos)):
                            act.wait_ge(S["ang_ready"], 2 * st.g + i + 1)
                            nc.scalar.activation(table[:, :, :], folded, ACT.Sin).then_inc(S["sin_ready"], 1)
                    for k in range(KC):
                        act.wait_ge(S["tr_full"], st.tr + k + 1)
                        nc.scalar.activation(hH[:, k, 0:nt * P], TR[(st.tr + k) % 2][:, 0:nt * P], ACT.Copy,
                                             scale=gcol[:, 0 if st.source == "mem" else 1, k:k + 1]).then_inc(S["h_hi"], 1)
                elif st.kind == "unit":
                    act.wait_ge(S["tile_done"], st.wt + 1)
                    if st.wt + 2 < len(units):
                        split_hi(st.wt + 2)
                    bank = PJ[st.u % 2][0:st.width, 0:st.n_tok]
                    if st.role in ("z", "mk", "cq", "gate") and st.x >= 2:
                        act.wait_ge(S["mixed"], st.x - 1)
                    if st.role in ("kv", "qi", "kiw", "q", "ak", "av", "mv"):
                        if st.f >= 2:
                            act.wait_ge(S["tr_full"], turn_r[st.f - 2] + 1)
                        if st.role == "q" and st.of == "b":
                            act.wait_ge(S["selected"], st.g + 1)
                        nc.scalar.activation(fT[0:st.width, st.f % 2, 0:st.n_tok], bank, ACT.Copy).then_inc(S["act_pj"], 1)
                    elif st.role in ("mk", "cq"):
                        hi = mKH[:, st.h, :] if st.role == "mk" else qst[:, st.i, :]
                        nc.scalar.activation(hi, bank, ACT.Copy)
                        nc.scalar.activation(ub[:, st.x % 2, 0:st.n_tok], bank, ACT.Copy).then_inc(S["act_pj"], 1)
                    elif st.role == "z":
                        nc.scalar.activation(sg[:, st.x % 2, :], bank, ACT.Sigmoid)
                        nc.scalar.activation(ub[:, st.x % 2, :], bank, ACT.Copy).then_inc(S["act_pj"], 1)
                    elif st.role == "gate":
                        nc.scalar.activation(sg[:, st.x % 2, :], bank, ACT.Sigmoid).then_inc(S["act_pj"], 1)
                    elif st.role == "up":
                        nc.scalar.activation(ub[:, st.x % 2, :], bank, ACT.Copy).then_inc(S["act_pj"], 1)
                    elif st.role == "out":
                        nc.scalar.activation(ob[:, st.m, :], bank, ACT.Copy).then_inc(S["act_pj"], 1)
                elif st.kind == "turn":
                    turn_r.append(st.tr)
                elif st.kind == "restack":
                    un = st.unit
                    act.wait_ge(S["roped"], st.k + 1)
                    if st.k:
                        act.wait_ge(S["tr_full"], st.before)
                    nh = 1 if un.role in ("kv", "kiw") else 2
                    if un.role in ("q", "kiw"):
                        last = nc.scalar.activation(stack_view(0, nh)[:, :, 0, :], t1_heads(nh), ACT.Copy)
                    else:
                        last = nc.scalar.activation(stack_view(0, nh), twice(t1_heads(nh), NT * nh), ACT.Copy)
                    last.then_inc(S["stack_hi"], 1)
                elif st.kind == "index":
                    for tt, h, c, size, s, n in st.parts:
                        act.wait_ge(S["s_full"], s + 1)
                        if n >= 2:
                            act.wait_ge(S["rel_used"], n - 1)
                        nc.scalar.activation(rel[:, n % 2, 0:size], SC[s % 2][:, 0:size], ACT.Relu).then_inc(S["act_s"], 1)
                elif st.kind == "attention":
                    act.wait_ge(S["mixed"], st.x)
                    exps(st.items[0], st.branch, st.keys)
                    for i, it in enumerate(st.items):
                        if i + 1 < len(st.items):
                            exps(st.items[i + 1], st.branch, st.keys)
                        turned_hi(it)
                elif st.kind == "split_y":
                    act.wait_ge(S["dve_pj"], st.used)
                    nc.scalar.activation(ysH[:, :, :], zs[:, :, :], ACT.Copy).then_inc(S["y_hi"], 1)
                elif st.kind == "split_m":
                    act.wait_ge(S["mixed"], st.x)
                    for half in range(2):
                        nc.scalar.activation(hH[:, 4 * half:4 * half + 4, :], merged[:, 4 * half:4 * half + 4, :],
                                             ACT.Copy).then_inc(S["m_hi"], 1)
                elif st.kind == "finish":
                    act.wait_ge(S["tr_free"], st.tr + 2 * NT)
                    squares(NT)
                    n_root += 1
                    root(n_root, NT)

        @block.gpsimd
        def _(pool):
            done = [0]

            def link(ins):
                done[0] += 1
                ins.then_inc(S["pool_step"], 1)
                pool.wait_ge(S["pool_step"], done[0])

            def split_lo(wt):
                un = units[wt]
                pool.wait_ge(S["hi_ready"], wt + 1)
                b, k, c = wt % 2, un.kc, un.width
                nc.gpsimd.tensor_tensor(wL[:, b, 0:k, 0:c], raw[:, b, 0:k, 0:c], wH[:, b, 0:k, 0:c].bitcast(F32),
                                        ALU.subtract).then_inc(S["lo_ready"], 1)

            link(nc.gpsimd.memset(ident[:, :], 0.0))
            link(nc.gpsimd.affine_select(out=ident[:, :], in_=ident[:, :], compare_op=ALU.not_equal, fill=1.0,
                                         base=0, pattern=[[-1, P]], channel_multiplier=1))
            link(nc.gpsimd.memset(wmask[:, :, :], 0.0))
            link(nc.gpsimd.memset(wmask[0:64, 0, 0:128], MASKED))
            link(nc.gpsimd.memset(wmask[0:64, 1, 0:64], MASKED))
            link(nc.gpsimd.memset(wmask[0:64, :, 192:256], MASKED))
            link(nc.gpsimd.memset(wmask[64:128, :, 0:128], MASKED))
            freq = np.power(np.float32(THETA), -np.arange(32, dtype=np.float32) * 2 / HD).astype(np.float32)
            for j in range(32):
                link(nc.gpsimd.memset(inv[:, j:j + 1], float(freq[j])))
            link(nc.gpsimd.memset(vS[:, 0:HD].bitcast(F32), 0.0))
            link(nc.gpsimd.memset(wv[:, 0:HD + 2 * P].bitcast(F32), 0.0))
            link(nc.gpsimd.memset(wkA[:, :, 0:P].bitcast(F32), 0.0))
            nc.gpsimd.memset(wkB[:, :, 0:P].bitcast(F32), 0.0).then_inc(S["consts"], 1)
            split_lo(0)
            split_lo(1)
            for st in steps:
                if st.kind == "unit":
                    if st.wt + 2 < len(units):
                        split_lo(st.wt + 2)
                    if st.role in ("mk", "cq", "z", "up"):
                        pool.wait_ge(S["act_pj"], st.evac)
                        a, b = sg[:, st.x % 2, 0:st.n_tok], ub[:, st.x % 2, 0:st.n_tok]
                    if st.role == "mk":
                        nc.gpsimd.tensor_tensor(mKL[:, st.h, :], b, mKH[:, st.h, :].bitcast(F32), ALU.subtract).then_inc(S["mixed"], 1)
                    elif st.role == "cq":
                        nc.gpsimd.tensor_tensor(qst[:, 4 + st.i, :], b, qst[:, st.i, :].bitcast(F32), ALU.subtract).then_inc(S["mixed"], 1)
                    elif st.role == "z":
                        if st.y:
                            pool.wait_ge(S["y_hi"], st.y)
                        if st.g:
                            pool.wait_ge(S["out_ready"], st.g)
                        nc.gpsimd.tensor_tensor(zs[:, st.i, :], a, b, ALU.mult).then_inc(S["mixed"], 1)
                    elif st.role == "up" and st.first:
                        nc.gpsimd.tensor_tensor(merged[:, st.m, :], a, b, ALU.mult).then_inc(S["mixed"], 1)
                    elif st.role == "up":
                        link(nc.gpsimd.tensor_tensor(b, a, b, ALU.mult))
                        nc.gpsimd.tensor_tensor(merged[:, st.m, :], merged[:, st.m, :], b, ALU.add).then_inc(S["mixed"], 1)
                elif st.kind == "restack":
                    un = st.unit
                    pool.wait_ge(S["stack_hi"], st.k + 1)
                    nh = 1 if un.role in ("kv", "kiw") else 2
                    hi = stack_view(0, nh).bitcast(F32)
                    if un.role in ("q", "kiw"):
                        last = nc.gpsimd.tensor_tensor(stack_view(0, nh)[:, :, 1, :], t1_heads(nh), hi[:, :, 0, :], ALU.subtract)
                    else:
                        last = nc.gpsimd.tensor_tensor(stack_view(1, nh), twice(t1_heads(nh), NT * nh), hi, ALU.subtract)
                    last.then_inc(S["stack_lo"], 1)
                elif st.kind == "split_y":
                    pool.wait_ge(S["y_hi"], st.y + 1)
                    nc.gpsimd.tensor_tensor(ysL[:, :, :], zs[:, :, :], ysH[:, :, :].bitcast(F32), ALU.subtract).then_inc(S["y_lo"], 1)
                elif st.kind == "split_m":
                    for half in range(2):
                        pool.wait_ge(S["m_hi"], 2 * st.g + half + 1)
                        ms = slice(4 * half, 4 * half + 4)
                        last = nc.gpsimd.tensor_tensor(hL[:, ms, :], merged[:, ms, :], hH[:, ms, :].bitcast(F32), ALU.subtract)
                    last.then_inc(S["m_lo"], 1)

        @block.vector
        def _(dve):
            done = [0]

            def link(ins):
                done[0] += 1
                ins.then_inc(S["dve_step"], 1)
                dve.wait_ge(S["dve_step"], done[0])

            TT, TS, STT = nc.vector.tensor_tensor, nc.vector.tensor_scalar, nc.vector.scalar_tensor_tensor
            n_root, n_squares = [0], [0]

            def inverse_rms(tiles):
                n_root[0] += 1
                n_squares[0] += tiles
                dve.wait_ge(S["squared"], n_squares[0])
                v, q, t = var[:, 0:tiles], rstd[:, 0:tiles], tmp[:, 0:tiles]
                TS(v, ssq[:, 0:tiles], 1.0 / D, EPS, ALU.mult, ALU.add).then_inc(S["var_ready"], 1)
                dve.wait_ge(S["rooted"], n_root[0])
                link(nc.vector.reciprocal(q, q))
                link(TT(t, q, q, ALU.mult))
                link(TT(t, t, v, ALU.mult))
                link(TS(t, t, -0.5, 1.5, ALU.mult, ALU.add))
                link(TT(q, q, t, ALU.mult))

            def cut(value, n_bits):
                m, e = np.frexp(value)
                return float(np.floor(m * 2 ** n_bits) / 2 ** n_bits * 2.0 ** e)

            def tables(g):
                full, parts = 2 * np.pi, []
                for n_bits in (8, 9, 9):
                    parts.append(cut(full, n_bits))
                    full -= parts[-1]
                parts.append(float(np.float32(full)))
                at_tok = posf[:, g * NT:(g + 1) * NT].unsqueeze(2).broadcast_to([P, NT, 32])
                link(TT(ang, at_tok, inv[:, :].unsqueeze(1).broadcast_to([P, NT, 32]), ALU.mult))
                magic = 1.5 * 2.0 ** 23
                for i in range(2):
                    link(TS(turns, ang, 0.5 / np.pi, 0.25 * i, ALU.mult, ALU.add))
                    link(TS(turns, turns, magic, -magic, ALU.add, ALU.add))
                    if i:
                        dve.wait_ge(S["sin_ready"], 2 * g + 1)
                    link(STT(folded, turns, -parts[0], ang, ALU.mult, ALU.add))
                    for c in parts[1:]:
                        link(STT(folded, turns, -c, folded, ALU.mult, ALU.add))
                    if i:
                        link(TS(folded, folded, np.pi / 2, None, ALU.add))
                    TS(folded, folded, 3.1415925, -3.1415925, ALU.min, ALU.max).then_inc(S["ang_ready"], 1)

            def rope(un, tr, k):
                bank = TR[tr % 2]
                dve.wait_ge(S["tr_full"], tr + 1)
                cols = bank[:, 0:NT * P].rearrange("p (t c) -> p t c", t=NT)
                nh = 1 if un.role in ("kv", "kiw") else 2
                if k:
                    dve.wait_ge(S["stack_hi"], k)
                    dve.wait_ge(S["stack_lo"], k)
                if un.role == "kv":
                    dst = vS[:, HD + un.g * T:HD + (un.g + 1) * T].rearrange("p (t c) -> p t c", t=NT)
                    link(nc.vector.tensor_copy(dst[:, :, 0:HD], cols[:, :, HD:P]))
                    TT(dst[:, :, HD:P], cols[:, :, HD:P], dst[:, :, 0:HD].bitcast(F32), ALU.subtract)
                elif un.role == "kiw":
                    TS(wi[:, :, :], cols[:, :, HD:HD + 4], 2.0 ** -4, None, ALU.mult)
                n = 2 * nh
                src4 = cols[:, :, 0:nh * HD].rearrange("p t (n c) -> p t n c", c=32)
                t1v = t1[:, 0:NT * nh * HD].rearrange("p (t n c) -> p t n c", t=NT, c=32)
                t2v = t2[:, 0:NT * nh * HD].rearrange("p (t n c) -> p t n c", t=NT, c=32)
                TT(t1v, src4, tabled(cos, n), ALU.mult)
                for half in range(2):
                    step = TT(t2v[:, :, half::2, :], src4[:, :, 1 - half::2, :], tabled(sin, nh), ALU.mult)
                    if half:
                        step.then_inc(S["tr_free"], 1)
                dve.wait_ge(S["tr_free"], tr + 1)
                a, b = (t[:, 0:NT * nh * HD].rearrange("p (n a c) -> p n a c", a=2, c=32) for t in (t1, t2))
                TT(a[:, :, 0, :], a[:, :, 0, :], b[:, :, 0, :], ALU.subtract)
                TT(a[:, :, 1, :], a[:, :, 1, :], b[:, :, 1, :], ALU.add).then_inc(S["roped"], 1)

            def put(tr, dst):
                dve.wait_ge(S["tr_full"], tr + 1)
                nc.vector.tensor_copy(dst, TR[tr % 2][:, :]).then_inc(S["tr_free"], 1)

            def window_values(un, tr):
                dve.wait_ge(S["tr_full"], tr + 1)
                if un.role == "av":
                    dst = wv[:, HD + 2 * P:HD + 10 * P].rearrange("p (n c) -> p n c", c=P)
                    src = TR[tr % 2][:, :].rearrange("p (n c) -> p n c", c=HD)
                    hi, lo = dst[:, :, 0:HD], dst[:, :, HD:P]
                else:
                    src = TR[tr % 2][:, 0:MEM].rearrange("p (n c) -> p n c", c=P)
                    hi, lo = (m[:, :, un.h * P:(un.h + 1) * P] for m in (mVH, mVL))
                link(nc.vector.tensor_copy(hi, src))
                TT(lo, src, hi.bitcast(F32), ALU.subtract).then_inc(S["tr_free"], 1)

            def front(it, branch, g):
                a = it.a % 2
                slot = prob[:, a, :]
                if branch == "b":
                    for i, (c, size, s) in enumerate(it.chunks):
                        dve.wait_ge(S["s_full"], s + 1)
                        nc.vector.tensor_tensor_reduce(slot[:, c:c + size], SC[s % 2][:, 0:size],
                                                       score[:, it.tt, c:c + size], 1.0, LOWEST, ALU.add,
                                                       ALU.max, top[:, 2 * a + i:2 * a + i + 1]).then_inc(S["dve_s"], 1)
                    dve.wait_ge(S["dve_s"], s_freed[s][1])
                    if len(it.chunks) == 2:
                        link(TT(top[:, 2 * a:2 * a + 1], top[:, 2 * a:2 * a + 1], top[:, 2 * a + 1:2 * a + 2], ALU.max))
                    TS(nmx[:, a, 0:1], top[:, 2 * a:2 * a + 1], -HD ** -0.5, None, ALU.mult).then_inc(S["p_sub"], 1)
                    return
                s = it.chunks[0][2]
                dve.wait_ge(S["s_full"], s + 1)
                sc = SC[s % 2][:, :].rearrange("p (t c) -> p t c", t=NT)
                pr = slot[:, 0:1024].rearrange("p (t c) -> p t c", t=NT)
                if branch == "a":
                    if g == 0:
                        TT(pr[:, 0, :], sc[:, 0, :], wmask[:, 0, :], ALU.add)
                        link(TT(pr[:, 1:NT, :], sc[:, 1:NT, :], wmask[:, 1, :].unsqueeze(1).broadcast_to([P, NT - 1, 256]), ALU.add))
                    else:
                        link(TT(pr, sc, wmask[:, 1, :].unsqueeze(1).broadcast_to([P, NT, 256]), ALU.add))
                    src = pr
                else:
                    src = sc
                link(nc.vector.tensor_reduce(top[:, :], src, AX.X, ALU.max))
                if branch == "a":
                    link(TS(top[:, :], top[:, :], sink8[:, it.h:it.h + 1], None, ALU.max))
                    TS(snk[:, a, :], top[:, :], -1.0, sink8[:, it.h:it.h + 1], ALU.mult, ALU.add)
                TT(pr, src, top[:, :].unsqueeze(2).broadcast_to([P, NT, 256]), ALU.subtract).then_inc(S["dve_s"], 1)
                dve.wait_ge(S["dve_s"], s_freed[s][1])
                dve.sem_inc(S["p_sub"], 1)

            def middle(it, branch, keys):
                a = it.a % 2
                slot = prob[:, a, :]
                dve.wait_ge(S["p_exp"], it.a + 1)
                if branch == "b":
                    link(nc.vector.reciprocal(rden[:, 0:1], psum[:, a, 0:1]))
                    TS(slot[:, 0:keys], slot[:, 0:keys], rden[:, 0:1], None, ALU.mult).then_inc(S["p_ready"], 1)
                    return
                pr = slot[:, 0:1024].rearrange("p (t c) -> p t c", t=NT)
                link(nc.vector.tensor_reduce(den[:, :], pr, AX.X, ALU.add))
                if branch == "a":
                    link(TT(den[:, :], den[:, :], esnk[:, a, :], ALU.add))
                link(nc.vector.reciprocal(rden[:, :], den[:, :]))
                TT(pr, pr, rden[:, :].unsqueeze(2).broadcast_to([P, NT, 256]), ALU.mult).then_inc(S["p_ready"], 1)

            def back(it, branch, seen):
                for j in range(it.groups):
                    tr, p = it.tr + j, it.p + j
                    dve.wait_ge(S["pt_hi"], p + 1)
                    TT(ptL[:, p % 2, :], TR[tr % 2][:, :], ptH[:, p % 2, :].bitcast(F32), ALU.subtract).then_inc(S["tr_free"], 1)
                dve.wait_ge(S["pv_done"], it.p + it.groups)
                if branch == "c":
                    rows, tile, tok = slice(0, P), it.h, slice(0, T)
                else:
                    rows, tile = slice(HD * (it.h % 2), HD * (it.h % 2) + HD), it.h // 2
                    tok = slice(0, T) if it.tt is None else slice(it.tt * P, (it.tt + 1) * P)
                z = zs[rows, tile, tok]
                TT(z, PJ[it.u % 2][rows, 0:tok.stop - tok.start], z, ALU.mult).then_inc(S["dve_pj"], 1)

            def select(g, keys):
                n = keys
                flags, ranks = prob[:, 0, 0:n], prob[:, 1, 0:n]

                def as_float(bits_in):
                    link(TS(flip, bits_in, 31, 0x7FFFFFFF, ALU.arith_shift_right, ALU.bitwise_xor))
                    link(STT(thr, flip, -2 ** 31, bits_in, ALU.bitwise_or, ALU.bitwise_xor))

                link(nc.vector.memset(ubits, 0))
                for bit in range(31, -1, -1):
                    one = 1 << bit if bit < 31 else -2 ** 31
                    link(TS(cand, ubits, one, None, ALU.bitwise_or))
                    as_float(cand)
                    for b in range(NT):
                        link(TS(flags, score[:, b, 0:n], thr.bitcast(F32)[:, b:b + 1], 0.0, ALU.is_ge, ALU.add,
                                accum_out=cnt[:, b:b + 1]))
                    link(TS(gi, cnt, TOPK - 0.5, None, ALU.is_ge))
                    link(STT(ubits, gi, bit, ubits, ALU.logical_shift_left, ALU.bitwise_or))
                as_float(ubits)
                t = thr.bitcast(F32)
                for b in range(NT):
                    link(TS(flags, score[:, b, 0:n], t[:, b:b + 1], 0.0, ALU.is_gt, ALU.add, accum_out=cnt[:, b:b + 1]))
                link(TS(need, cnt, -1.0, float(TOPK), ALU.mult, ALU.add))
                for b in range(NT):
                    sc = score[:, b, 0:n]
                    link(TS(flags, sc, t[:, b:b + 1], None, ALU.is_equal))
                    link(nc.vector.tensor_tensor_scan(ranks, flags, flags, 0.0, ALU.add, ALU.max))
                    link(STT(flags, ranks, need[:, b:b + 1], flags, ALU.is_le, ALU.mult))
                    link(STT(flags, sc, t[:, b:b + 1], flags, ALU.is_gt, ALU.add))
                    link(TS(sc, flags, -1.0, -MASKED, ALU.add, ALU.mult))
                    last = bar(g, b, keys, MASKED)
                link(last)
                dve.sem_inc(S["selected"], 1)

            def bar(g, tt, keys, value):
                for half in range(2):
                    first = g * T + tt * P + (half + 1) * CHUNK
                    if first < keys:
                        last = nc.vector.memset(score[half * 64:half * 64 + 64, tt, first:keys], value)
                return last

            dve.wait_ge(S["small_in"], 64)
            dve.wait_ge(S["consts"], 1)
            link(nc.vector.tensor_copy(posf[:, :], posi[:, :]))
            link(TS(sink8[:, :], sink[:, :], HD ** 0.5, None, ALU.mult))
            for st in steps:
                if st.kind == "norm":
                    n, nt = norms.index(st), 2 if st.source == "mem" else NT
                    inverse_rms(nt)
                    for t in range(nt):
                        last = TS(xs[:, t, :], xs[:, t, :], rstd[:, t:t + 1], None, ALU.mult)
                    last.then_inc(S["scaled"], 1)
                    if st.source == "x":
                        tables(st.g)
                    for k in range(KC):
                        dve.wait_ge(S["h_hi"], n * KC + k + 1)
                        STT(hL[:, k, 0:nt * P], TR[(st.tr + k) % 2][:, 0:nt * P],
                            gcol[:, 0 if st.source == "mem" else 1, k:k + 1], hH[:, k, 0:nt * P].bitcast(F32),
                            ALU.mult, ALU.subtract).then_inc(S["tr_free"], 1)
                elif st.kind == "turn":
                    un = st.unit
                    if un.role == "kv":
                        dve.wait_ge(S["sin_ready"], 2 * un.g + 2)
                    if un.role == "ak" and un.g:
                        nc.vector.tensor_copy(wkA[:, :, 0:P], wkA[:, :, T:T + P].bitcast(F32))
                        nc.vector.tensor_copy(wkB[:, :, 0:P], wkB[:, :, T:T + P].bitcast(F32))
                        nc.vector.tensor_copy(wv[:, HD:HD + 2 * P], wv[:, HD + NT * 2 * P:HD + (NT + 1) * 2 * P].bitcast(F32))
                    if un.role in ("av", "mv"):
                        window_values(un, st.tr)
                    else:
                        rope(un, st.tr, un.k)
                elif st.kind == "restack":
                    un = st.unit
                    tok = slice(un.g * T, (un.g + 1) * T)
                    if un.role == "kv":
                        to = [kA[:, tok], kB[:, tok]]
                    elif un.role == "kiw":
                        to = [kiS[:, tok]]
                    elif un.role == "ak":
                        to = [wkA[:, 0, P:], wkA[:, 1, P:], wkB[:, 0, P:], wkB[:, 1, P:]]
                    elif un.role == "q":
                        to = [qst[:, 2 * un.i + h, :] for h in range(2)]
                    else:
                        to = [qst[:, 4 * i + 2 * un.i + h, :] for i in range(2) for h in range(2)]
                    for j, dst in enumerate(to):
                        put(st.tr + j, dst)
                elif st.kind == "index":
                    for tt, h, c, size, s, m in st.parts:
                        dve.wait_ge(S["act_s"], s_freed[s][1])
                        sc, rl, wt = score[:, tt, c:c + size], rel[:, m % 2, 0:size], wi[:, tt, h:h + 1]
                        if h == 0:
                            ins = TS(sc, rl, wt, None, ALU.mult)
                        else:
                            ins = STT(sc, rl, wt, sc, ALU.mult, ALU.add)
                        ins.then_inc(S["rel_used"], 1)
                        dve.wait_ge(S["rel_used"], m + 1)
                        if h == 3 and c + size == st.keys:
                            link(bar(st.g, tt, st.keys, LOWEST))
                elif st.kind == "select":
                    select(st.g, st.keys)
                elif st.kind == "attention":
                    dve.wait_ge(S["mixed"], st.x)
                    front(st.items[0], st.branch, st.g)
                    for i, it in enumerate(st.items):
                        if i + 1 < len(st.items):
                            front(st.items[i + 1], st.branch, st.g)
                        middle(it, st.branch, st.keys)
                        back(it, st.branch, None)
                elif st.kind == "finish":
                    dve.wait_ge(S["x_in"], 16 * (3 + 2 * st.g))
                    for j in range(2 * NT):
                        tt, half = divmod(j, 2)
                        dve.wait_ge(S["tr_full"], st.tr + j + 1)
                        row = xs[:, tt, half * T:(half + 1) * T]
                        TT(row, TR[(st.tr + j) % 2][:, :], row, ALU.add).then_inc(S["tr_free"], 1)
                    inverse_rms(NT)
                    dve.wait_ge(S["gfin_in"], 16 * (st.g + 1))
                    for t in range(NT):
                        last = STT(xs[:, t, :], xs[:, t, :], rstd[:, t:t + 1], gfin[:, :], ALU.mult, ALU.mult)
                    last.then_inc(S["out_ready"], 1)


_INS = ["x", "mem", "positions", "g_in", "w_in", "attn_sinks", "g_mem", "w_mem_kv", "w_branch", "w_out", "g_final"]


def kernel(**inputs):
    import concourse.bacc as bacc
    from concourse.bass_utils import run_bass_kernel_spmd

    nc = bacc.Bacc("TRN2", target_bir_lowering=False, num_devices=1, dynamic_dma_scratch_size=1024)
    arrays, args = {}, []
    for name in _INS:
        a = np.asarray(inputs[name])
        if name in ("positions", "g_in", "g_mem"):
            a = a.reshape(-1, P).T
        a = np.ascontiguousarray(a)
        arrays[f"in_{name}"] = a
        args.append(nc.dram_tensor(f"in_{name}", a.shape, mybir.dt.from_np(a.dtype), kind="ExternalInput").ap())
    out = nc.dram_tensor("out", (1, SEQ, D), F32, kind="ExternalOutput").ap()
    hybrid_block(nc, *args, out)
    result = run_bass_kernel_spmd(nc, [arrays], core_ids=[0])
    return result.results[0]["out"]
```

```python
from contextlib import ExitStack

import numpy as np
import concourse.bass as bass
from concourse import mybir

F32, F32R, I32 = mybir.dt.float32, mybir.dt.float32r, mybir.dt.int32
ALU = mybir.AluOpType
ACT = mybir.ActivationFunctionType
AX = mybir.AxisListType

P = 128
D, SEQ, MEM = 1024, 2048, 256
KC = D // P
BW = D // 2
BC = BW // P
T = 512
NG = SEQ // T
NT = T // P
CHUNK, HD = 64, 64
TOPK = 256
EPS = 1e-6
THETA = 10000.0
MASKED = -1e30
LOWEST = -3.4028234663852886e38

A_Q, A_K, A_V, A_Z = 0, 512, 640, 768
B_Q, B_KV, B_QI, B_KIW, B_Z = 1280, 1792, 1920, 2176, 2244
C_Q, C_Z, GATES = 2756, 3268, 3780


class Step:

    def __init__(self, kind, role=None, source=None, src=None, which=None, branch=None, g=None, i=None,
                 h=None, m=None, tt=None, of=None, n=None, col=None, kc=None, width=None, moving=None, n_tok=None,
                 first=None, keys=None, chunks=None, groups=None, items=None, parts=None, unit=None,
                 wt=None, u=None, evac=None, used=None, f=None, x=None, y=None, k=None, a=None, tr=None,
                 p=None, before=None, turn_r=None):
        self.kind = kind
        self.role, self.source, self.src, self.which, self.branch, self.g = role, source, src, which, branch, g
        self.i, self.h, self.m, self.tt, self.of, self.col = i, h, m, tt, of, col
        self.kc, self.width, self.moving, self.n_tok, self.first, self.keys = kc, width, moving, n_tok, first, keys
        self.chunks, self.groups, self.items, self.parts, self.unit, self.wt = chunks, groups, items, parts, unit, wt
        self.u, self.evac, self.used, self.f, self.x, self.y = u, evac, used, f, x, y
        self.k, self.a, self.tr, self.p, self.before, self.turn_r, self.n = k, a, tr, p, before, turn_r, n


def order_of_work():
    steps = []
    n = dict(wt=0, u=0, tr=0, s=0, f=0, x=0, k=0, a=0, y=0, rel=0, p=0, stacked=0, b_items=0, ac_items=0, ups=0)
    count = dict(act_pj=0, dve_pj=0, act_s=0, dve_s=0)
    pj_freed, s_freed = [], []
    last_out = None

    def take(name, k=1):
        n[name] += k
        return n[name] - k

    def freed(ring, engine, of):
        count[f"{engine}_{of}"] += 1
        ring.append((engine, count[f"{engine}_{of}"]))

    def unit(role, src, col, kc=KC, width=P, moving="h", n_tok=T, **more):
        st = Step("unit", role=role, src=src, col=col, kc=kc, width=width, moving=moving,
                  n_tok=n_tok, wt=take("wt"), u=take("u"), **more)
        freed(pj_freed, "act", "pj")
        st.evac = pj_freed[-1][1]
        if role in ("kv", "qi", "kiw", "q", "ak", "av", "mv"):
            st.f = take("f")
        if role in ("z", "mk", "cq", "gate"):
            st.x = take("x")
        if role == "up":
            st.x = n["x"] - 2
            take("u")
            freed(pj_freed, "act", "pj")
            st.n = take("ups")
        steps.append(st)
        return st

    def turned(specs):
        units = []
        for k in range(len(specs) + 2):
            if k < len(specs):
                role, src, col, more = specs[k]
                units.append(unit(role, src, col, **more))
            if k >= 2:
                st = units[k - 2]
                banks = {"kv": 2, "qi": 4, "kiw": 1, "q": 2, "ak": 4}.get(st.role, 0)
                if banks:
                    steps.append(Step("restack", unit=st, tr=take("tr", banks), k=st.k, before=n["stacked"]))
                    n["stacked"] = n["tr"]
            if 1 <= k <= len(specs):
                st = units[k - 1]
                if st.role not in ("av", "mv"):
                    st.k = take("k")
                steps.append(Step("turn", unit=st, tr=take("tr")))
                st.turn_r = steps[-1].tr

    def prepare(source, g):
        steps.append(Step("prepare", source=source, g=g, used=count["dve_pj"]))

    def finish(g):
        steps.append(Step("finish", g=g, tr=take("tr", 2 * NT), y=last_out.y, evac=last_out.evac))

    def norm(source, g):
        steps.append(Step("norm", source=source, g=g, tr=take("tr", KC)))

    def attention(branch, g):
        if branch == "b":
            items, keys = [(tt, h) for tt in range(NT) for h in range(8)], T * (g + 1)
            chunks = [(c, min(1024, keys - c)) for c in range(0, keys, 1024)]
        else:
            items, keys = [(None, h) for h in range(4 if branch == "c" else 8)], 256
            chunks = [(0, NT * 256)]
        group = Step("attention", branch=branch, g=g, keys=keys, items=[])
        group.n = min(4, 3 * SEQ // keys) if branch == "b" else 2
        for tt, h in items:
            it = Step("item", tt=tt, h=h, a=take("a"), u=take("u"), chunks=[])
            it.i = len(group.items) % group.n
            it.keys = keys
            freed(pj_freed, "dve", "pj")
            it.used = pj_freed[-1][1]
            it.n = take("b_items" if branch == "b" else "ac_items")
            for c, size in chunks:
                it.chunks.append((c, size, take("s")))
                if branch == "b":
                    freed(s_freed, "dve", "s")
                else:
                    s_freed.append(("exp", it.a + 1))
            it.groups = keys // T if branch == "b" else 2
            it.tr, it.p = take("tr", it.groups), take("p", it.groups)
            group.items.append(it)
        group.x = n["x"]
        steps.append(group)

    bits = iter(range(31, -1, -1))

    def select_bits(g, k):
        for _ in range(k):
            steps.append(Step("bit", g=g, keys=T * (g + 1), i=next(bits)))

    def branch(which, g):
        steps.append(Step("split_y", y=take("y"), used=count["dve_pj"]))
        for m in range(0, KC, 2):
            for i in range(2):
                unit("gate", "w_in", GATES + which * D + (m + i) * P, m=m + i)
            unit("up", "w_branch", m * P, kc=BC, width=2 * P, moving="y", m=m, which=which, y=n["y"],
                 first=(which == 2), g=g)
            if which != 1:
                select_bits(g, 2)
            elif m == 2 and g + 1 < NG:
                prepare("x", g + 1)

    prepare("mem", 0)
    norm("mem", 0)
    for h in range(4):
        unit("mk", "w_mem_kv", h * P, n_tok=MEM, h=h)
    turned([("mv", "w_mem_kv", BW + h * P, dict(n_tok=MEM, h=h)) for h in range(4)])
    steps.append(Step("save_mem", x=n["x"], tr=n["tr"]))
    prepare("x", 0)
    for g in range(NG):
        bits = iter(range(31, -1, -1))
        norm("x", g)
        turned([("kv", "w_in", B_KV, dict(g=g)),
                ("qi", "w_in", B_QI, dict(g=g, i=0)),
                ("qi", "w_in", B_QI + P, dict(g=g, i=1)),
                ("kiw", "w_in", B_KIW, dict(g=g, width=HD + 4))])
        if g:
            finish(g - 1)
        st = Step("index", g=g, keys=T * (g + 1), parts=[], tr=n["tr"])
        for tt in range(NT):
            for h in range(4):
                for c in range(0, st.keys, 1024):
                    st.parts.append((tt, h, c, min(1024, st.keys - c), take("s"), take("rel")))
                    freed(s_freed, "act", "s")
        steps.append(st)
        for i in range(4):
            unit("z", "w_in", C_Z + i * P, i=i, g=g, y=n["y"])
            if i % 2:
                select_bits(g, 1)
        for i in range(4):
            unit("cq", "w_in", C_Q + i * P, i=i)
            if i % 2:
                select_bits(g, 1)
        attention("c", g)
        branch(2, g)
        for i in range(4):
            unit("z", "w_in", A_Z + i * P, i=i, g=g, y=n["y"])
            if i % 2:
                select_bits(g, 1)
        turned([("ak", "w_in", A_K, dict(g=g, y=n["y"])), ("av", "w_in", A_V, dict(g=g))]
               + [("q", "w_in", A_Q + i * P, dict(g=g, i=i, of="a")) for i in range(4)])
        attention("a", g)
        branch(0, g)
        for i in range(4):
            unit("z", "w_in", B_Z + i * P, i=i, g=g, y=n["y"])
        select_bits(g, 10)
        steps.append(Step("select", g=g, keys=T * (g + 1)))
        turned([("q", "w_in", B_Q + i * P, dict(g=g, i=i, of="b")) for i in range(4)])
        attention("b", g)
        branch(1, g)
        steps.append(Step("split_m", g=g, x=n["x"], y=n["y"]))
        for m in range(KC):
            last_out = unit("out", "w_out", m * P, moving="m", m=m, g=g, y=n["y"])
    finish(NG - 1)
    return steps, pj_freed, s_freed, n


def hybrid_block(nc, x, mem, positions, g_in, w_in, attn_sinks, g_mem, w_mem_kv, w_branch, w_out,
                 g_final, out):
    steps, pj_freed, s_freed, _ = order_of_work()
    x_v = x[0].rearrange("(g t p) d -> g p t d", t=NT, p=P)
    out_v = out[0].rearrange("(g t p) d -> g p t d", t=NT, p=P)
    mem_v = mem[0].rearrange("(t p) d -> p t d", p=P)
    weights = {"w_in": w_in[0].rearrange("(k p) n -> p k n", p=P),
               "w_mem_kv": w_mem_kv[0].rearrange("(k p) n -> p k n", p=P),
               "w_out": w_out[0].rearrange("(k p) n -> p k n", p=P)}
    up_v = w_branch[0].rearrange("b (k p) n -> b p k n", p=P)
    mem_scratch = nc.dram_tensor("mem_scratch", (P, 4096), F32, kind="Internal").ap()

    ctx = ExitStack()
    with ctx:
        at = [(nc.sbuf_base + 63) // 64 * 64]

        def sb(name, shape, dt=F32, offset=None):
            size = int(np.prod(shape[1:])) * (1 if dt == mybir.dt.uint8 else 4)
            if offset is None:
                offset, at[0] = at[0], at[0] + (size + 31) // 32 * 32
            return nc.alloc_sbuf_tensor_at(name, shape, dt, offset=offset)

        def region(size):
            at[0] += size
            return at[0] - size

        def sem(name):
            return ctx.enter_context(nc.semaphore(name))

        hH, hL = sb("hH", [P, KC, T], F32R), sb("hL", [P, KC, T], F32R)
        raw, wH, wL = (sb(n, [P, 2, KC, P], d) for n, d in (("raw", F32), ("wH", F32R), ("wL", F32R)))
        kA, kB, kiS = (sb(n, [P, SEQ], F32R) for n in ("kA", "kB", "kiS"))
        vS = sb("vS", [P, SEQ // P, 3, HD], F32R)
        ckA, ckB, cv = (sb(n, [P, 2, P], F32R) for n in ("ckA", "ckB", "cv"))
        score_at = region(NT * SEQ * 4)
        score = sb("score", [P, NT, SEQ], offset=score_at)
        squared_rows = sb("squared_rows", [P, D], offset=score_at + SEQ * 4)
        rows = sb("rows", [P, NT, D], offset=score_at + 2 * SEQ * 4)
        merged_at = region(16384)
        merged = sb("merged", [P, KC, T], offset=merged_at)
        ob = sb("ob", [P, KC, T], offset=merged_at)
        memkv = sb("memkv", [P, 4096], F32R, offset=merged_at)
        ys_at = region(16384)
        ysH, ysL = sb("ysH", [P, BC, T], F32R, ys_at), sb("ysL", [P, BC, T], F32R, ys_at + 8192)
        wkA, wkB = (sb(n, [P, 2, P + T], F32R, ys_at + o) for n, o in (("wkA", 0), ("wkB", 5120)))
        wv = sb("wv", [P, HD + (NT + 1) * 2 * P], F32R, ys_at + 10240)
        zs_at = region(8192)
        zs = sb("zs", [P, BC, T], offset=zs_at)
        gfin = sb("gfin", [P, D], offset=zs_at)
        qst_at = region(16384)
        qst = sb("qst", [P, 8, T], F32R, offset=qst_at)
        junk = sb("junk", [P, D], offset=qst_at)
        p_at = region(3 * SEQ * 4)
        prob = sb("prob", [P, 3, SEQ], offset=p_at)
        xs = sb("xs", [P, NT, D], offset=p_at)
        fT = sb("fT", [P, 2, T], offset=p_at)
        t1 = sb("t1", [P, T], offset=p_at + 4096)
        t2 = sb("t2", [P, T], offset=p_at + 6144)
        stack = sb("stack", [P, 2, 1024], F32R, offset=p_at + 8192)
        rel = sb("rel", [P, 2, 1024], offset=p_at + 8192)
        pt_at = region(8192)
        ptH = sb("ptH", [P, 2, T], F32R, offset=pt_at)
        ptL = sb("ptL", [P, 2, T], F32R, offset=pt_at + 4096)
        sg = sb("sg", [P, 2, T], offset=pt_at)
        ub = sb("ub", [P, 2, T], offset=pt_at + 4096)
        above_at = region(SEQ)
        above = sb("above", [P, SEQ], mybir.dt.uint8, offset=above_at)
        made = sb("made", [P, P], offset=above_at)
        rsum = sb("rsum", [P, 2 * P], offset=above_at + 512)
        cos, sin = sb("cos", [P, NT, 32]), sb("sin", [P, NT, 32])
        wmask = sb("wmask", [P, 2, 256], F32R)
        identR = sb("identR", [P, P], F32R)
        wi = sb("wi", [P, NT, 4])
        inv = sb("inv", [P, 32])
        posi, posf = sb("posi", [P, SEQ // P], I32), sb("posf", [P, SEQ // P])
        gcol = sb("gcol", [P, 2, KC])
        sink = sb("sink", [P, 8])
        small = sb("small", [P, 6, NT])
        ssq, var, rstd, tmp, cnt, need = (small[:, i, :] for i in range(6))
        rden, top, den = (sb(n, [P, 2, NT]) for n in ("rden", "top", "den"))
        snk, esnk, nmx, psum = (sb(n, [P, 2, NT]) for n in ("snk", "esnk", "nmx", "psum"))
        bits = sb("bits", [P, 5, NT], I32)
        ubits, cand, flip, thr, gi = (bits[:, i, :] for i in range(5))
        assert at[0] <= nc.sbuf_usable_end, at[0]
        ang, turns, folded = (score[:, 0, i * 128:(i + 1) * 128].rearrange("p (t j) -> p t j", t=NT) for i in range(3))

        def t1_heads(nh):
            return t1[:, 0:NT * nh * HD].rearrange("p (n c) -> p n c", c=HD)

        def held(it, branch, of=None):
            size = it.keys if branch == "b" else SEQ
            return prob[:, :, :].rearrange("p a c -> p (a c)")[:, it.i * size:it.i * size + (it.keys if branch == "b" else 1024)]

        def stack_view(which, nh):
            return stack[:, which, 0:NT * nh * P].rearrange("p (n a c) -> p n a c", a=2, c=HD)

        def twice(ap, n):
            return ap.unsqueeze(2).broadcast_to([P, n, 2, HD])

        def tabled(table, n):
            return table[:, :, :].unsqueeze(2).broadcast_to([P, NT, n, 32])
        mKH = memkv[:, 0:1024].rearrange("p (h m) -> p h m", h=4)
        mKL = memkv[:, 1024:2048].rearrange("p (h m) -> p h m", h=4)
        mVH = memkv[:, 2048:3072].rearrange("p (t n) -> p t n", t=2)
        mVL = memkv[:, 3072:4096].rearrange("p (t n) -> p t n", t=2)

        PJ = [ctx.enter_context(nc.psum_tensor(f"PJ{i}", [P, T], F32)) for i in range(2)]
        TR = [ctx.enter_context(nc.psum_tensor(f"TR{i}", [P, T], F32)) for i in range(2)]
        SC = [ctx.enter_context(nc.psum_tensor(f"SC{i}", [P, 1024], F32)) for i in range(2)]

        names = """x_in rows_in half_done pos_in small_in gfin_in raw_in0 raw_in1 mem_out mem_in store
            hi_ready lo_ready tile_done act_pj dve_pj y_done tr_full tr_free s_full act_s dve_s
            pv_done stack_hi stack_lo roped rel_used mixed y_hi y_lo m_hi m_lo p_sub p_exp p_ready p_ready_ac rden_ready
            pt_hi h_hi squared var_ready rooted scaled selected out_ready consts dve_step pool_step
            act_step tables_in sin_ready ang_ready""".split()
        S = {n: sem(n) for n in names}
        raw_in = [S["raw_in0"], S["raw_in1"]]
        block = ctx.enter_context(nc.Block())
        freed_by = {"exp_s": S["p_exp"], "act_pj": S["act_pj"], "dve_pj": S["dve_pj"], "act_s": S["act_s"], "dve_s": S["dve_s"]}

        units = [st for st in steps if st.kind == "unit"]

        def tile_of(ring, un):
            c = 2 * P if un.role == "up" else P
            flat = ring[:, un.wt % 2, :, :].rearrange("p k c -> p (k c)")
            return flat[:, 0:un.kc * c].rearrange("p (k c) -> p k c", c=c)[:, :, 0:un.width]
        norms = [st for st in steps if st.kind == "norm"]

        def wait_bank(eng, ring, index, of):
            if index >= 2:
                engine, value = ring[index - 2]
                eng.wait_ge(freed_by[f"{engine}_{of}"], value)

        @block.sync
        def _(sp):
            def load_tile(wt):
                if wt >= 2:
                    sp.wait_ge(S["lo_ready"], wt - 1)
                st = units[wt]
                src = up_v[st.which] if st.src == "w_branch" else weights[st.src]
                sp.dma_start(tile_of(raw, st), src[:, :, st.col:st.col + st.width]).then_inc(raw_in[wt % 2], 16)

            sp.dma_start(xs[:, 0:2, :], mem_v).then_inc(S["x_in"], 16)
            sp.dma_start(posi[:, :], positions).then_inc(S["small_in"], 16)
            sp.dma_start(gcol[:, 0, :], g_mem).then_inc(S["small_in"], 16)
            sp.dma_start(gcol[:, 1, :], g_in).then_inc(S["small_in"], 16)
            sp.dma_start(sink[:, :], attn_sinks.broadcast_to([P, 8])).then_inc(S["small_in"], 16)
            load_tile(0)
            load_tile(1)
            loads = 1
            for st in steps:
                if st.kind == "prepare" and st.source == "x":
                    if st.g:
                        sp.wait_ge(S["dve_pj"], st.used)
                    else:
                        sp.wait_ge(S["mem_out"], 16)
                    sp.dma_start(xs[:, :, :], x_v[st.g]).then_inc(S["x_in"], 16)
                elif st.kind == "save_mem":
                    sp.wait_ge(S["mixed"], st.x)
                    sp.wait_ge(S["tr_free"], st.tr)
                    sp.dma_start(mem_scratch, memkv[:, :].bitcast(F32)).then_inc(S["mem_out"], 16)
                elif st.kind == "unit":
                    if st.wt + 2 < len(units):
                        load_tile(st.wt + 2)
                elif st.kind == "split_m":
                    sp.wait_ge(S["y_lo"], st.y)
                    sp.dma_start(rows[:, :, :], x_v[st.g]).then_inc(S["rows_in"], 16)
                    sp.dma_start(gfin[:, :], g_final.unsqueeze(0).broadcast_to([P, D])).then_inc(S["gfin_in"], 16)
                elif st.kind == "finish":
                    sp.wait_ge(S["out_ready"], st.g + 1)
                    sp.dma_start(out_v[st.g], rows[:, :, :]).then_inc(S["store"], 16)
                    if st.g + 1 < NG:
                        sp.wait_ge(S["tr_free"], st.tr + 2 * NT)
                        sp.dma_start(memkv[:, :].bitcast(F32), mem_scratch).then_inc(S["mem_in"], 16)
            sp.wait_ge(S["store"], 16 * NG)

        @block.tensor
        def _(pe):
            def transposes(tr, blocks, parts=False):
                if tr >= 2:
                    pe.wait_ge(S["tr_free"], tr - 1)
                for at_col, src in blocks:
                    k, m = src.shape[0], src.shape[1]
                    bank = TR[tr % 2][0:m, at_col:at_col + k]
                    if parts:
                        last = nc.tensor.transpose(bank.bitcast(F32R), src, identR[0:k, 0:k])
                    else:
                        last = nc.tensor.transpose(bank, src, identR[0:k, 0:k].bitcast(F32))
                last.then_inc(S["tr_full"], 1)

            def scores(it, branch, g, chunks=(0, 1)):
                for c, size, s in [it.chunks[i] for i in chunks if i < len(it.chunks)]:
                    wait_bank(pe, s_freed, s, "s")
                    bank = SC[s % 2]
                    if branch == "b":
                        lhs = qst[:, it.h, it.tt * P:(it.tt + 1) * P]
                        for o in range(0, size, 512):
                            nc.tensor.matmul(bank[:, o:o + 512], lhs, kA[:, c + o:c + o + 512], start=True, stop=False)
                            last = nc.tensor.matmul(bank[:, o:o + 512], lhs, kB[:, c + o:c + o + 512], start=False, stop=True)
                    for tt in range(NT):
                        o = tt * 256
                        tok = slice(tt * P, (tt + 1) * P)
                        if branch == "a":
                            lhs, kv = qst[:, it.h, tok], it.h // 4
                            keys = slice(tt * P, tt * P + 256)
                            nc.tensor.matmul(bank[:, o:o + 256], identR[:, :], wmask[:, 0 if g == 0 and tt == 0 else 1, :],
                                             start=True, stop=False)
                            nc.tensor.matmul(bank[:, o:o + 256], lhs, wkA[:, kv, keys], start=False, stop=False)
                            last = nc.tensor.matmul(bank[:, o:o + 256], lhs, wkB[:, kv, keys], start=False, stop=True)
                        elif branch == "c":
                            qh, ql = qst[:, it.h, tok], qst[:, 4 + it.h, tok]
                            nc.tensor.matmul(bank[:, o:o + 256], qh, mKH[:, it.h, :], start=True, stop=False)
                            nc.tensor.matmul(bank[:, o:o + 256], qh, mKL[:, it.h, :], start=False, stop=False)
                            last = nc.tensor.matmul(bank[:, o:o + 256], ql, mKH[:, it.h, :], start=False, stop=True)
                    last.then_inc(S["s_full"], 1)

            def turned(it, branch, j):
                slot = held(it, branch)
                if j == 0:
                    if branch == "b":
                        pe.wait_ge(S["p_exp"], it.a + 1)
                    else:
                        pe.wait_ge(S["p_ready_ac"], it.n + 1)
                if branch == "b":
                    cols = [(4 * j + i) * P for i in range(4)]
                else:
                    cols = [tt * 256 + j * P for tt in range(NT)]
                transposes(it.tr + j, [(i * P, slot[:, c:c + P]) for i, c in enumerate(cols)])

            def products(it, branch, j):
                if j == 0:
                    wait_bank(pe, pj_freed, it.u, "pj")
                pe.wait_ge(S["tr_free"], it.tr + j + 1)
                H, L = ptH[:, (it.p + j) % 2, :], ptL[:, (it.p + j) % 2, :]
                bank, odd = PJ[it.u % 2], it.h % 2
                end = j == it.groups - 1
                for b in range(1 if branch == "c" else 4):
                    p = slice(b * P, (b + 1) * P)
                    if branch == "c":
                        vh, vl = mVH[:, j, it.h * P:(it.h + 1) * P], mVL[:, j, it.h * P:(it.h + 1) * P]
                        col, p = slice(0, T), slice(0, T)
                    elif branch == "b":
                        v = vS[:, 4 * j + b, :, :].rearrange("p a c -> p (a c)")
                        vh, vl = v[:, 0:P], v[:, P:P + HD]
                        col = slice(0, P)
                    else:
                        base, col = ((b + j) * 2 + it.h // 4) * P, p
                        vh = wv[:, base:base + P] if odd else wv[:, HD + base:2 * HD + base]
                        vl = wv[:, HD + base:HD + base + P] if odd else wv[:, 2 * HD + base:3 * HD + base]
                    last_block = end and (branch != "b" or b == 3)
                    for i, (v, pr) in enumerate(((vh, H), (vl, H), (vh, L))):
                        m = HD if (branch == "a" and not odd) or (branch == "b" and i == 1) else P
                        last = nc.tensor.matmul(bank[0:m, col], v, pr[:, p], start=(j == 0 and b == 0 and i == 0),
                                                stop=(last_block and i == 2), skip_group_check=True)
                last.then_inc(S["pv_done"], 1)

            pe.wait_ge(S["consts"], 1)
            for st in steps:
                if st.kind == "norm":
                    nt = 2 if st.source == "mem" else NT
                    pe.wait_ge(S["scaled"], norms.index(st) + 1)
                    for k in range(KC):
                        transposes(st.tr + k, [(t * P, xs[:, t, k * P:(k + 1) * P]) for t in range(nt)])
                    pe.wait_ge(S["tr_free"], st.tr + KC)
                elif st.kind == "unit":
                    pe.wait_ge(S["lo_ready"], st.wt + 1)
                    if st.moving == "y":
                        pe.wait_ge(S["y_lo"], st.y)
                    if st.moving == "m":
                        pe.wait_ge(S["m_lo"], st.g + 1)
                    mH, mL = (ysH, ysL) if st.moving == "y" else (hH, hL)
                    vH, vL = tile_of(wH, st), tile_of(wL, st)
                    halves = 2 if st.role == "up" else 1
                    for half in range(halves):
                        wait_bank(pe, pj_freed, st.u + half, "pj")
                        cols = slice(half * P, min((half + 1) * P, st.width))
                        o = PJ[(st.u + half) % 2][0:cols.stop - cols.start, 0:st.n_tok]
                        for k in range(st.kc):
                            for i, (lhs, rhs) in enumerate(((vH, mH), (vH, mL), (vL, mH))):
                                last = nc.tensor.matmul(o, lhs[:, k, cols], rhs[:, k, 0:st.n_tok],
                                                        start=(k == 0 and i == 0), stop=(k == st.kc - 1 and i == 2))
                        last.then_inc(S["tile_done" if half == halves - 1 else "half_done"], 1)
                elif st.kind == "turn":
                    un = st.unit
                    pe.wait_ge(S["act_pj"], un.evac)
                    src = fT[:, un.f % 2, :]
                    transposes(st.tr, [(t * P, src[0:un.width, t * P:(t + 1) * P]) for t in range(un.n_tok // P)])
                elif st.kind == "restack":
                    un = st.unit
                    pe.wait_ge(S["stack_lo"], st.k + 1)
                    nh = {"kv": 1, "kiw": 1}.get(un.role, 2)
                    for j in range({"kv": 2, "qi": 4, "kiw": 1, "q": 2, "ak": 4}[un.role]):
                        which, h = divmod(j, nh)
                        transposes(st.tr + j, [(t * P, stack[:, which, (t * nh + h) * P:(t * nh + h + 1) * P])
                                              for t in range(NT)], parts=True)
                elif st.kind == "index":
                    pe.wait_ge(S["tr_free"], st.tr)
                    for tt, h, c, size, s, _ in st.parts:
                        wait_bank(pe, s_freed, s, "s")
                        for o in range(0, size, 512):
                            for i in range(2):
                                last = nc.tensor.matmul(SC[s % 2][:, o:o + 512], qst[:, 4 * i + h, tt * P:(tt + 1) * P],
                                                        kiS[:, c + o:c + o + 512], start=(i == 0), stop=(i == 1))
                        last.then_inc(S["s_full"], 1)
                elif st.kind == "attention":
                    if st.branch == "c":
                        pe.wait_ge(S["mixed"], st.x)
                        if st.g:
                            pe.wait_ge(S["mem_in"], 16 * st.g)
                    else:
                        pe.wait_ge(S["tr_free"], st.items[0].tr)
                    items, branch = st.items, st.branch
                    scores(items[0], branch, st.g)
                    scores(items[1], branch, st.g)
                    behind = None
                    for i, it in enumerate(items):
                        for j in range(it.groups):
                            turned(it, branch, j)
                            if behind:
                                products(behind[0], branch, behind[1])
                            behind = (it, j)
                            if i + 2 < len(items):
                                scores(items[i + 2], branch, st.g, [c for c in range(2) if min(2 * c, it.groups - 1) == j])
                    if behind:
                        products(behind[0], branch, behind[1])
                elif st.kind == "finish":
                    pe.wait_ge(S["act_pj"], st.evac)
                    for j in range(2 * NT):
                        tt, half = divmod(j, 2)
                        transposes(st.tr + j, [(m * P, ob[:, 4 * half + m, tt * P:(tt + 1) * P]) for m in range(4)])

        @block.scalar
        def _(act):
            def split_hi(wt):
                un = units[wt]
                act.wait_ge(raw_in[wt % 2], 16 * (wt // 2 + 1))
                if wt >= 2:
                    act.wait_ge(S["tile_done"], wt - 1)
                nc.scalar.activation(tile_of(wH, un), tile_of(raw, un), ACT.Copy).then_inc(S["hi_ready"], 1)

            n_squares = [0]

            def squares(tiles, src, junk):
                for t in range(tiles):
                    if n_squares[0]:
                        act.wait_ge(S["squared"], n_squares[0])
                    n_squares[0] += 1
                    nc.scalar.activation(junk[:, :], src[:, t, :], ACT.Square,
                                         accum_out=ssq[:, t:t + 1]).then_inc(S["squared"], 1)

            def root(n, tiles):
                act.wait_ge(S["var_ready"], n)
                nc.scalar.activation(rstd[:, 0:tiles], var[:, 0:tiles], ACT.Sqrt).then_inc(S["rooted"], 1)

            def exps(it, branch, keys):
                act.wait_ge(S["p_sub"], it.a + 1)
                scale = (P if branch == "c" else HD) ** -0.5
                slot = held(it, branch)
                if branch == "b":
                    nc.scalar.activation(slot, slot, ACT.Exp, bias=nmx[:, it.a % 2, 0:1],
                                         scale=scale).then_inc(S["p_exp"], 1)
                else:
                    if branch == "a":
                        nc.scalar.activation(esnk[:, it.a % 2, :], snk[:, it.a % 2, :], ACT.Exp)
                    bank = SC[it.chunks[0][2] % 2]
                    for tt in range(NT):
                        cols = slice(tt * 256, tt * 256 + 256)
                        last = nc.scalar.activation(slot[:, cols], bank[:, cols], ACT.Exp, bias=nmx[:, it.a % 2, tt:tt + 1],
                                                    scale=scale, accum_out=psum[:, it.a % 2, tt:tt + 1])
                    last.then_inc(S["p_exp"], 1)

            def turned_hi(it, j):
                tr, p = it.tr + j, it.p + j
                act.wait_ge(S["tr_full"], tr + 1)
                if p >= 2:
                    act.wait_ge(S["pv_done"], p - 1)
                nc.scalar.activation(ptH[:, p % 2, :], TR[tr % 2][:, :], ACT.Copy).then_inc(S["pt_hi"], 1)

            turn_r = []
            n_prepared = n_root = 0
            split_hi(0)
            split_hi(1)
            for st in steps:
                if st.kind == "prepare":
                    n_prepared += 1
                    nt = 2 if st.source == "mem" else NT
                    if n_prepared == 1:
                        act.wait_ge(S["small_in"], 64)
                    act.wait_ge(S["x_in"], 16 * n_prepared)
                    squares(nt, xs, junk)
                    n_root += 1
                    root(n_root, nt)
                    if st.source == "x":
                        for i, table in enumerate((sin, cos)):
                            act.wait_ge(S["ang_ready"], 2 * st.g + i + 1)
                            nc.scalar.activation(table[:, :, :], folded, ACT.Sin).then_inc(S["sin_ready"], 1)
                elif st.kind == "norm":
                    nt = 2 if st.source == "mem" else NT
                    for k in range(KC):
                        act.wait_ge(S["tr_full"], st.tr + k + 1)
                        nc.scalar.activation(hH[:, k, 0:nt * P], TR[(st.tr + k) % 2][:, 0:nt * P], ACT.Copy,
                                             scale=gcol[:, 0 if st.source == "mem" else 1, k:k + 1]).then_inc(S["h_hi"], 1)
                elif st.kind == "unit":
                    if st.role == "up":
                        act.wait_ge(S["half_done"], st.n + 1)
                        nc.scalar.activation(ub[:, st.x % 2, :], PJ[st.u % 2][:, :], ACT.Copy).then_inc(S["act_pj"], 1)
                    act.wait_ge(S["tile_done"], st.wt + 1)
                    if st.wt + 2 < len(units):
                        split_hi(st.wt + 2)
                    bank = PJ[st.u % 2][0:min(st.width, P), 0:st.n_tok]
                    if st.role in ("z", "mk", "cq", "gate") and st.x >= 2:
                        act.wait_ge(S["mixed"], st.x - 1)
                    if st.role in ("kv", "qi", "kiw", "q", "ak", "av", "mv"):
                        if st.f >= 2:
                            act.wait_ge(S["tr_full"], turn_r[st.f - 2] + 1)
                        if st.role == "q" and st.of == "b":
                            act.wait_ge(S["selected"], st.g + 1)
                        nc.scalar.activation(fT[0:st.width, st.f % 2, 0:st.n_tok], bank, ACT.Copy).then_inc(S["act_pj"], 1)
                    elif st.role in ("mk", "cq"):
                        hi = mKH[:, st.h, :] if st.role == "mk" else qst[:, st.i, :]
                        nc.scalar.activation(hi, bank, ACT.Copy)
                        nc.scalar.activation(ub[:, st.x % 2, 0:st.n_tok], bank, ACT.Copy).then_inc(S["act_pj"], 1)
                    elif st.role == "z":
                        nc.scalar.activation(sg[:, st.x % 2, :], bank, ACT.Sigmoid)
                        nc.scalar.activation(ub[:, st.x % 2, :], bank, ACT.Copy).then_inc(S["act_pj"], 1)
                    elif st.role == "gate":
                        nc.scalar.activation(sg[:, st.x % 2, :], bank, ACT.Sigmoid).then_inc(S["act_pj"], 1)
                    elif st.role == "up":
                        nc.scalar.activation(ub[:, (st.x + 1) % 2, :], PJ[(st.u + 1) % 2][:, :], ACT.Copy).then_inc(S["act_pj"], 1)
                    elif st.role == "out":
                        nc.scalar.activation(ob[:, st.m, :], bank, ACT.Copy).then_inc(S["act_pj"], 1)
                elif st.kind == "turn":
                    turn_r.append(st.tr)
                elif st.kind == "restack":
                    un = st.unit
                    act.wait_ge(S["roped"], st.k + 1)
                    if st.k:
                        act.wait_ge(S["tr_full"], st.before)
                    nh = 1 if un.role in ("kv", "kiw") else 2
                    if un.role in ("q", "kiw"):
                        last = nc.scalar.activation(stack_view(0, nh)[:, :, 0, :], t1_heads(nh), ACT.Copy)
                    else:
                        last = nc.scalar.activation(stack_view(0, nh), twice(t1_heads(nh), NT * nh), ACT.Copy)
                    last.then_inc(S["stack_hi"], 1)
                elif st.kind == "index":
                    for tt, h, c, size, s, n in st.parts:
                        act.wait_ge(S["s_full"], s + 1)
                        if n >= 2:
                            act.wait_ge(S["rel_used"], n - 1)
                        nc.scalar.activation(rel[:, n % 2, 0:size], SC[s % 2][:, 0:size], ACT.Relu).then_inc(S["act_s"], 1)
                elif st.kind == "attention":
                    act.wait_ge(S["mixed"], st.x)
                    items, b = st.items, st.branch == "b"
                    ahead = 1 if b else 2
                    for it in items[:ahead]:
                        exps(it, st.branch, st.keys)
                    for i, it in enumerate(items):
                        for j in range(it.groups):
                            turned_hi(it, j)
                            if j == min(1, it.groups - 1) and i + ahead < len(items):
                                exps(items[i + ahead], st.branch, st.keys)
                elif st.kind == "split_y":
                    act.wait_ge(S["dve_pj"], st.used)
                    nc.scalar.activation(ysH[:, :, :], zs[:, :, :], ACT.Copy).then_inc(S["y_hi"], 1)
                elif st.kind == "split_m":
                    act.wait_ge(S["mixed"], st.x)
                    for half in range(2):
                        nc.scalar.activation(hH[:, 4 * half:4 * half + 4, :], merged[:, 4 * half:4 * half + 4, :],
                                             ACT.Copy).then_inc(S["m_hi"], 1)
                elif st.kind == "finish":
                    act.wait_ge(S["tr_free"], st.tr + 2 * NT)
                    squares(NT, rows, squared_rows)
                    n_root += 1
                    root(n_root, NT)

        @block.gpsimd
        def _(pool):
            done = [0]

            def link(ins):
                done[0] += 1
                ins.then_inc(S["pool_step"], 1)
                pool.wait_ge(S["pool_step"], done[0])

            def split_lo(wt):
                un = units[wt]
                pool.wait_ge(S["hi_ready"], wt + 1)
                nc.gpsimd.tensor_tensor(tile_of(wL, un), tile_of(raw, un), tile_of(wH, un).bitcast(F32), ALU.subtract).then_inc(S["lo_ready"], 1)

            link(nc.gpsimd.memset(made[:, :], 0.0))
            link(nc.gpsimd.affine_select(out=made[:, :], in_=made[:, :], compare_op=ALU.not_equal, fill=1.0,
                                         base=0, pattern=[[-1, P]], channel_multiplier=1))
            link(nc.gpsimd.tensor_copy(identR[:, :], made[:, :]))
            link(nc.gpsimd.memset(wmask[:, :, :].bitcast(F32), 0.0))
            link(nc.gpsimd.memset(wmask[0:64, 0, 0:128].bitcast(F32), MASKED))
            link(nc.gpsimd.memset(wmask[0:64, 1, 0:64].bitcast(F32), MASKED))
            link(nc.gpsimd.memset(wmask[0:64, :, 192:256].bitcast(F32), MASKED))
            link(nc.gpsimd.memset(wmask[64:128, :, 0:128].bitcast(F32), MASKED))
            freq = np.power(np.float32(THETA), -np.arange(32, dtype=np.float32) * 2 / HD).astype(np.float32)
            for j in range(32):
                link(nc.gpsimd.memset(inv[:, j:j + 1], float(freq[j])))
            link(nc.gpsimd.memset(vS[:, :, 1, :].bitcast(F32), 1.0))
            for carried in (ckA, ckB, cv):
                last = nc.gpsimd.memset(carried[:, :, :].bitcast(F32), 0.0)
            last.then_inc(S["consts"], 1)
            split_lo(0)
            split_lo(1)
            for st in steps:
                if st.kind == "unit":
                    if st.wt + 2 < len(units):
                        split_lo(st.wt + 2)
                    if st.role in ("mk", "cq", "z"):
                        pool.wait_ge(S["act_pj"], st.evac)
                        a, b = sg[:, st.x % 2, 0:st.n_tok], ub[:, st.x % 2, 0:st.n_tok]
                    if st.role == "mk":
                        nc.gpsimd.tensor_tensor(mKL[:, st.h, :], b, mKH[:, st.h, :].bitcast(F32), ALU.subtract).then_inc(S["mixed"], 1)
                    elif st.role == "cq":
                        nc.gpsimd.tensor_tensor(qst[:, 4 + st.i, :], b, qst[:, st.i, :].bitcast(F32), ALU.subtract).then_inc(S["mixed"], 1)
                    elif st.role == "z":
                        if st.y:
                            pool.wait_ge(S["y_hi"], st.y)
                        if st.g:
                            pool.wait_ge(S["out_ready"], st.g)
                        nc.gpsimd.tensor_tensor(zs[:, st.i, :], a, b, ALU.mult).then_inc(S["mixed"], 1)
                    elif st.role == "up":
                        for half in range(2):
                            pool.wait_ge(S["act_pj"], st.evac + half)
                            a, b = sg[:, (st.x + half) % 2, :], ub[:, (st.x + half) % 2, :]
                            sum_m = merged[:, st.m + half, :]
                            if st.first:
                                nc.gpsimd.tensor_tensor(sum_m, a, b, ALU.mult).then_inc(S["mixed"], 1)
                            else:
                                link(nc.gpsimd.tensor_tensor(b, a, b, ALU.mult))
                                nc.gpsimd.tensor_tensor(sum_m, sum_m, b, ALU.add).then_inc(S["mixed"], 1)
                elif st.kind == "restack":
                    un = st.unit
                    pool.wait_ge(S["stack_hi"], st.k + 1)
                    nh = 1 if un.role in ("kv", "kiw") else 2
                    hi = stack_view(0, nh).bitcast(F32)
                    if un.role in ("q", "kiw"):
                        last = nc.gpsimd.tensor_tensor(stack_view(0, nh)[:, :, 1, :], t1_heads(nh), hi[:, :, 0, :], ALU.subtract)
                    else:
                        last = nc.gpsimd.tensor_tensor(stack_view(1, nh), twice(t1_heads(nh), NT * nh), hi, ALU.subtract)
                    last.then_inc(S["stack_lo"], 1)
                elif st.kind == "attention" and st.branch != "b":
                    for it in st.items:
                        pool.wait_ge(S["rden_ready"], it.n + 1)
                        pr = held(it, st.branch).rearrange("p (t c) -> p t c", t=NT)
                        nc.gpsimd.tensor_tensor(pr, pr, rden[:, it.a % 2, :].unsqueeze(2).broadcast_to([P, NT, 256]),
                                                ALU.mult).then_inc(S["p_ready_ac"], 1)
                elif st.kind == "split_y":
                    pool.wait_ge(S["y_hi"], st.y + 1)
                    nc.gpsimd.tensor_tensor(ysL[:, :, :], zs[:, :, :], ysH[:, :, :].bitcast(F32), ALU.subtract).then_inc(S["y_lo"], 1)
                elif st.kind == "split_m":
                    for half in range(2):
                        pool.wait_ge(S["m_hi"], 2 * st.g + half + 1)
                        ms = slice(4 * half, 4 * half + 4)
                        last = nc.gpsimd.tensor_tensor(hL[:, ms, :], merged[:, ms, :], hH[:, ms, :].bitcast(F32), ALU.subtract)
                    last.then_inc(S["m_lo"], 1)

        @block.vector
        def _(dve):
            done = [0]

            def link(ins):
                done[0] += 1
                ins.then_inc(S["dve_step"], 1)
                dve.wait_ge(S["dve_step"], done[0])

            TT, TS, STT = nc.vector.tensor_tensor, nc.vector.tensor_scalar, nc.vector.scalar_tensor_tensor
            n_root, n_squares = [0], [0]

            def inverse_rms(tiles):
                n_root[0] += 1
                n_squares[0] += tiles
                dve.wait_ge(S["squared"], n_squares[0])
                v, q, t = var[:, 0:tiles], rstd[:, 0:tiles], tmp[:, 0:tiles]
                TS(v, ssq[:, 0:tiles], 1.0 / D, EPS, ALU.mult, ALU.add).then_inc(S["var_ready"], 1)
                dve.wait_ge(S["rooted"], n_root[0])
                link(nc.vector.reciprocal(q, q))
                link(TT(t, q, q, ALU.mult))
                link(TT(t, t, v, ALU.mult))
                link(TS(t, t, -0.5, 1.5, ALU.mult, ALU.add))
                link(TT(q, q, t, ALU.mult))

            def cut(value, n_bits):
                m, e = np.frexp(value)
                return float(np.floor(m * 2 ** n_bits) / 2 ** n_bits * 2.0 ** e)

            def tables(g):
                full, parts = 2 * np.pi, []
                for n_bits in (8, 9, 9):
                    parts.append(cut(full, n_bits))
                    full -= parts[-1]
                parts.append(float(np.float32(full)))
                at_tok = posf[:, g * NT:(g + 1) * NT].unsqueeze(2).broadcast_to([P, NT, 32])
                link(TT(ang, at_tok, inv[:, :].unsqueeze(1).broadcast_to([P, NT, 32]), ALU.mult))
                magic = 1.5 * 2.0 ** 23
                for i in range(2):
                    link(TS(turns, ang, 0.5 / np.pi, 0.25 * i, ALU.mult, ALU.add))
                    link(TS(turns, turns, magic, -magic, ALU.add, ALU.add))
                    if i:
                        dve.wait_ge(S["sin_ready"], 2 * g + 1)
                    link(STT(folded, turns, -parts[0], ang, ALU.mult, ALU.add))
                    for c in parts[1:]:
                        link(STT(folded, turns, -c, folded, ALU.mult, ALU.add))
                    if i:
                        link(TS(folded, folded, np.pi / 2, None, ALU.add))
                    TS(folded, folded, 3.1415925, -3.1415925, ALU.min, ALU.max).then_inc(S["ang_ready"], 1)

            def rope(un, tr, k):
                bank = TR[tr % 2]
                dve.wait_ge(S["tr_full"], tr + 1)
                cols = bank[:, 0:NT * P].rearrange("p (t c) -> p t c", t=NT)
                nh = 1 if un.role in ("kv", "kiw") else 2
                if k:
                    dve.wait_ge(S["stack_hi"], k)
                    dve.wait_ge(S["stack_lo"], k)
                if un.role == "kv":
                    hi, lo = (vS[:, un.g * NT:(un.g + 1) * NT, part, :] for part in (0, 2))
                    link(nc.vector.tensor_copy(hi, cols[:, :, HD:P]))
                    TT(lo, cols[:, :, HD:P], hi.bitcast(F32), ALU.subtract)
                elif un.role == "kiw":
                    TS(wi[:, :, :], cols[:, :, HD:HD + 4], 2.0 ** -4, None, ALU.mult)
                n = 2 * nh
                src4 = cols[:, :, 0:nh * HD].rearrange("p t (n c) -> p t n c", c=32)
                t1v = t1[:, 0:NT * nh * HD].rearrange("p (t n c) -> p t n c", t=NT, c=32)
                t2v = t2[:, 0:NT * nh * HD].rearrange("p (t n c) -> p t n c", t=NT, c=32)
                TT(t1v, src4, tabled(cos, n), ALU.mult)
                for half in range(2):
                    step = TT(t2v[:, :, half::2, :], src4[:, :, 1 - half::2, :], tabled(sin, nh), ALU.mult)
                    if half:
                        step.then_inc(S["tr_free"], 1)
                dve.wait_ge(S["tr_free"], tr + 1)
                a, b = (t[:, 0:NT * nh * HD].rearrange("p (n a c) -> p n a c", a=2, c=32) for t in (t1, t2))
                TT(a[:, :, 0, :], a[:, :, 0, :], b[:, :, 0, :], ALU.subtract)
                TT(a[:, :, 1, :], a[:, :, 1, :], b[:, :, 1, :], ALU.add).then_inc(S["roped"], 1)

            def put(tr, dst):
                dve.wait_ge(S["tr_full"], tr + 1)
                nc.vector.tensor_copy(dst, TR[tr % 2][:, :]).then_inc(S["tr_free"], 1)

            def window_values(un, tr):
                dve.wait_ge(S["tr_full"], tr + 1)
                if un.role == "av":
                    dst = wv[:, HD + 2 * P:HD + 10 * P].rearrange("p (n c) -> p n c", c=P)
                    src = TR[tr % 2][:, :].rearrange("p (n c) -> p n c", c=HD)
                    hi, lo = dst[:, :, 0:HD], dst[:, :, HD:P]
                else:
                    src = TR[tr % 2][:, 0:MEM].rearrange("p (n c) -> p n c", c=P)
                    hi, lo = (m[:, :, un.h * P:(un.h + 1) * P] for m in (mVH, mVL))
                link(nc.vector.tensor_copy(hi, src))
                TT(lo, src, hi.bitcast(F32), ALU.subtract).then_inc(S["tr_free"], 1)

            def masked(it, i):
                a = it.a % 2
                c, size, s = it.chunks[i]
                dve.wait_ge(S["s_full"], s + 1)
                nc.vector.tensor_tensor_reduce(held(it, "b")[:, c:c + size], SC[s % 2][:, 0:size],
                                               score[:, it.tt, c:c + size], 1.0, LOWEST, ALU.add,
                                               ALU.max, top[:, a, i:i + 1]).then_inc(S["dve_s"], 1)
                if i + 1 == len(it.chunks):
                    dve.wait_ge(S["dve_s"], s_freed[s][1])
                    highest = top[:, a, 0:1]
                    if i:
                        link(TT(highest, highest, top[:, a, 1:2], ALU.max))
                    TS(nmx[:, a, 0:1], highest, -HD ** -0.5, None, ALU.mult).then_inc(S["p_sub"], 1)

            def maxima(it, branch):
                a, s = it.a % 2, it.chunks[0][2]
                dve.wait_ge(S["s_full"], s + 1)
                sc = SC[s % 2][:, :].rearrange("p (t c) -> p t c", t=NT)
                link(nc.vector.tensor_reduce(top[:, a, :], sc, AX.X, ALU.max))
                if branch == "a":
                    link(TS(top[:, a, :], top[:, a, :], HD ** -0.5, sink[:, it.h:it.h + 1], ALU.mult, ALU.max))
                    link(TS(nmx[:, a, :], top[:, a, :], -1.0, None, ALU.mult))
                    TS(snk[:, a, :], nmx[:, a, :], sink[:, it.h:it.h + 1], None, ALU.add).then_inc(S["p_sub"], 1)
                else:
                    TS(nmx[:, a, :], top[:, a, :], -P ** -0.5, None, ALU.mult).then_inc(S["p_sub"], 1)

            def reciprocals(it, branch):
                a = it.a % 2
                dve.wait_ge(S["p_exp"], it.a + 1)
                sums = psum[:, a, :]
                if branch == "a":
                    link(TT(den[:, a, :], sums, esnk[:, a, :], ALU.add))
                    sums = den[:, a, :]
                nc.vector.reciprocal(rden[:, a, :], sums).then_inc(S["rden_ready"], 1)

            def turned_lo(it, j):
                tr, p = it.tr + j, it.p + j
                dve.wait_ge(S["pt_hi"], p + 1)
                TT(ptL[:, p % 2, :], TR[tr % 2][:, :], ptH[:, p % 2, :].bitcast(F32), ALU.subtract).then_inc(S["tr_free"], 1)

            def gated(it, branch):
                dve.wait_ge(S["pv_done"], it.p + it.groups)
                if branch == "c":
                    rows, tile, tok = slice(0, P), it.h, slice(0, T)
                else:
                    rows, tile = slice(HD * (it.h % 2), HD * (it.h % 2) + HD), it.h // 2
                    tok = slice(0, T) if it.tt is None else slice(it.tt * P, (it.tt + 1) * P)
                z = zs[rows, tile, tok]
                if branch == "b":
                    bank = PJ[it.u % 2]
                    link(nc.vector.reciprocal(rsum[0:HD, 0:P], bank[HD:P, 0:P]))
                    link(TT(rsum[rows, P:2 * P], bank[0:HD, 0:P], rsum[0:HD, 0:P], ALU.mult))
                    TT(z, z, rsum[rows, P:2 * P], ALU.mult).then_inc(S["dve_pj"], 1)
                    return
                TT(z, PJ[it.u % 2][rows, 0:tok.stop - tok.start], z, ALU.mult).then_inc(S["dve_pj"], 1)

            def as_float(bits_in):
                link(TS(flip, bits_in, 31, 0x7FFFFFFF, ALU.arith_shift_right, ALU.bitwise_xor))
                link(STT(thr, flip, -2 ** 31, bits_in, ALU.bitwise_or, ALU.bitwise_xor))

            def counts(keys, compare):
                for b in range(NT):
                    link(TS(above[:, 0:keys], score[:, b, 0:keys], thr.bitcast(F32)[:, b:b + 1], 0.0, compare, ALU.add,
                            accum_out=cnt[:, b:b + 1]))

            def threshold_bit(keys, bit):
                if bit == 31:
                    link(nc.vector.memset(ubits, 0))
                link(TS(cand, ubits, 1 << bit if bit < 31 else -2 ** 31, None, ALU.bitwise_or))
                as_float(cand)
                counts(keys, ALU.is_ge)
                link(TS(gi, cnt, TOPK - 0.5, None, ALU.is_ge))
                link(STT(ubits, gi, bit, ubits, ALU.logical_shift_left, ALU.bitwise_or))

            def select(g, keys):
                flags, ranks = prob[:, 0, 0:keys], prob[:, 1, 0:keys]
                as_float(ubits)
                t = thr.bitcast(F32)
                counts(keys, ALU.is_gt)
                link(TS(need, cnt, -1.0, float(TOPK), ALU.mult, ALU.add))
                for b in range(NT):
                    sc = score[:, b, 0:keys]
                    link(TS(flags, sc, t[:, b:b + 1], None, ALU.is_equal))
                    link(nc.vector.tensor_tensor_scan(ranks, flags, flags, 0.0, ALU.add, ALU.max))
                    link(STT(flags, ranks, need[:, b:b + 1], flags, ALU.is_le, ALU.mult))
                    link(STT(flags, sc, t[:, b:b + 1], flags, ALU.is_gt, ALU.add))
                    link(TS(sc, flags, -1.0, -MASKED, ALU.add, ALU.mult))
                    last = bar(g, b, keys, MASKED)
                link(last)
                dve.sem_inc(S["selected"], 1)

            def bar(g, tt, keys, value):
                for half in range(2):
                    first = g * T + tt * P + (half + 1) * CHUNK
                    if first < keys:
                        last = nc.vector.memset(score[half * 64:half * 64 + 64, tt, first:keys], value)
                return last

            dve.wait_ge(S["small_in"], 64)
            dve.wait_ge(S["consts"], 1)
            link(nc.vector.tensor_copy(posf[:, :], posi[:, :]))
            for st in steps:
                if st.kind == "prepare":
                    nt = 2 if st.source == "mem" else NT
                    inverse_rms(nt)
                    for t in range(nt):
                        last = TS(xs[:, t, :], xs[:, t, :], rstd[:, t:t + 1], None, ALU.mult)
                    last.then_inc(S["scaled"], 1)
                    if st.source == "x":
                        tables(st.g)
                elif st.kind == "norm":
                    n, nt = norms.index(st), 2 if st.source == "mem" else NT
                    for k in range(KC):
                        dve.wait_ge(S["h_hi"], n * KC + k + 1)
                        STT(hL[:, k, 0:nt * P], TR[(st.tr + k) % 2][:, 0:nt * P],
                            gcol[:, 0 if st.source == "mem" else 1, k:k + 1], hH[:, k, 0:nt * P].bitcast(F32),
                            ALU.mult, ALU.subtract).then_inc(S["tr_free"], 1)
                elif st.kind == "turn":
                    un = st.unit
                    if un.role == "kv":
                        dve.wait_ge(S["sin_ready"], 2 * un.g + 2)
                    if un.role == "ak":
                        dve.wait_ge(S["y_lo"], un.y)
                        dve.wait_ge(S["tr_full"], st.tr + 1)
                        nc.vector.tensor_copy(wkA[:, :, 0:P], ckA[:, :, :].bitcast(F32))
                        nc.vector.tensor_copy(wkB[:, :, 0:P], ckB[:, :, :].bitcast(F32))
                        nc.vector.tensor_copy(wv[:, HD:HD + 2 * P], cv[:, :, :].rearrange("p a c -> p (a c)").bitcast(F32))
                        nc.vector.memset(wv[:, 0:HD].bitcast(F32), 0.0)
                    if un.role in ("av", "mv"):
                        window_values(un, st.tr)
                    else:
                        rope(un, st.tr, un.k)
                elif st.kind == "restack":
                    un = st.unit
                    tok = slice(un.g * T, (un.g + 1) * T)
                    if un.role == "kv":
                        to = [kA[:, tok], kB[:, tok]]
                    elif un.role == "kiw":
                        to = [kiS[:, tok]]
                    elif un.role == "ak":
                        to = [wkA[:, 0, P:], wkA[:, 1, P:], wkB[:, 0, P:], wkB[:, 1, P:]]
                    elif un.role == "q":
                        to = [qst[:, 2 * un.i + h, :] for h in range(2)]
                    else:
                        to = [qst[:, 4 * i + 2 * un.i + h, :] for i in range(2) for h in range(2)]
                    for j, dst in enumerate(to):
                        put(st.tr + j, dst)
                elif st.kind == "index":
                    for tt, h, c, size, s, m in st.parts:
                        if st.g and (tt, h, c) == (1, 0, 0):
                            dve.wait_ge(S["store"], 16 * st.g)
                        dve.wait_ge(S["act_s"], s_freed[s][1])
                        sc, rl, wt = score[:, tt, c:c + size], rel[:, m % 2, 0:size], wi[:, tt, h:h + 1]
                        if h == 0:
                            ins = TS(sc, rl, wt, None, ALU.mult)
                        else:
                            ins = STT(sc, rl, wt, sc, ALU.mult, ALU.add)
                        ins.then_inc(S["rel_used"], 1)
                        dve.wait_ge(S["rel_used"], m + 1)
                        if h == 3 and c + size == st.keys:
                            link(bar(st.g, tt, st.keys, LOWEST))
                elif st.kind == "bit":
                    threshold_bit(st.keys, st.i)
                elif st.kind == "select":
                    select(st.g, st.keys)
                elif st.kind == "attention":
                    dve.wait_ge(S["mixed"], st.x)
                    items, branch = st.items, st.branch

                    def front(i, c):
                        if i < len(items) and c < len(items[i].chunks):
                            if branch == "b":
                                masked(items[i], c)
                            else:
                                maxima(items[i], branch)

                    for i in range(2):
                        front(i, 0)
                        front(i, 1)
                    if branch != "b":
                        reciprocals(items[0], branch)
                    for i, it in enumerate(items):
                        if branch != "b" and i + 1 < len(items):
                            reciprocals(items[i + 1], branch)
                        for j in range(it.groups):
                            turned_lo(it, j)
                            if j == 0 and i:
                                gated(items[i - 1], branch)
                            for c in range(2):
                                if min(2 * c + 1, it.groups - 1) == j:
                                    front(i + 2, c)
                    if branch == "a":
                        nc.vector.tensor_copy(ckA[:, :, :], wkA[:, :, T:T + P].bitcast(F32))
                        nc.vector.tensor_copy(ckB[:, :, :], wkB[:, :, T:T + P].bitcast(F32))
                        nc.vector.tensor_copy(cv[:, :, :].rearrange("p a c -> p (a c)"),
                                              wv[:, HD + NT * 2 * P:HD + (NT + 1) * 2 * P].bitcast(F32))
                    gated(items[-1], branch)
                elif st.kind == "finish":
                    dve.wait_ge(S["rows_in"], 16 * (st.g + 1))
                    for j in range(2 * NT):
                        tt, half = divmod(j, 2)
                        dve.wait_ge(S["tr_full"], st.tr + j + 1)
                        row = rows[:, tt, half * T:(half + 1) * T]
                        TT(row, TR[(st.tr + j) % 2][:, :], row, ALU.add).then_inc(S["tr_free"], 1)
                    inverse_rms(NT)
                    dve.wait_ge(S["gfin_in"], 16 * (st.g + 1))
                    for t in range(NT):
                        last = STT(rows[:, t, :], rows[:, t, :], rstd[:, t:t + 1], gfin[:, :], ALU.mult, ALU.mult)
                    last.then_inc(S["out_ready"], 1)


_INS = ["x", "mem", "positions", "g_in", "w_in", "attn_sinks", "g_mem", "w_mem_kv", "w_branch", "w_out", "g_final"]


def kernel(**inputs):
    import concourse.bacc as bacc
    from concourse.bass_utils import run_bass_kernel_spmd

    nc = bacc.Bacc("TRN2", target_bir_lowering=False, num_devices=1, dynamic_dma_scratch_size=1024)
    arrays, args = {}, []
    for name in _INS:
        a = np.asarray(inputs[name])
        if name in ("positions", "g_in", "g_mem"):
            a = a.reshape(-1, P).T
        a = np.ascontiguousarray(a)
        arrays[f"in_{name}"] = a
        args.append(nc.dram_tensor(f"in_{name}", a.shape, mybir.dt.from_np(a.dtype), kind="ExternalInput").ap())
    out = nc.dram_tensor("out", (1, SEQ, D), F32, kind="ExternalOutput").ap()
    hybrid_block(nc, *args, out)
    result = run_bass_kernel_spmd(nc, [arrays], core_ids=[0])
    return result.results[0]["out"]
```

```python
from contextlib import ExitStack

import numpy as np
import concourse.bass as bass
from concourse import mybir

F32, F32R, I32 = mybir.dt.float32, mybir.dt.float32r, mybir.dt.int32
ALU = mybir.AluOpType
ACT = mybir.ActivationFunctionType
AX = mybir.AxisListType

P = 128
D, SEQ, MEM = 1024, 2048, 256
KC = D // P
BW = D // 2
BC = BW // P
T = 512
NG = SEQ // T
NT = T // P
CHUNK, HD = 64, 64
TOPK = 256
EPS = 1e-6
THETA = 10000.0
MASKED = -1e30
LOWEST = -3.4028234663852886e38
PER_UNIT, PER_PAIR, PER_ITEM = (4, 4, 3, 2), (14, 13, 9, 7), (0, 0, 1, 2)

A_Q, A_K, A_V, A_Z = 0, 512, 640, 768
B_Q, B_KV, B_QI, B_KIW, B_Z = 1280, 1792, 1920, 2176, 2244
C_Q, C_Z, GATES = 2756, 3268, 3780


def admissible(g, tt):
    return max(TOPK, g * T + (tt + 1) * P)


def chunked(keys):
    n = 1 if keys <= 1024 else 2
    return [(c * (keys // n), keys // n) for c in range(n)]


class Step:

    def __init__(self, kind, role=None, source=None, src=None, which=None, branch=None, g=None, i=None,
                 h=None, m=None, tt=None, of=None, n=None, col=None, kc=None, width=None, moving=None, n_tok=None,
                 first=None, keys=None, chunks=None, groups=None, items=None, parts=None, unit=None,
                 wt=None, u=None, evac=None, used=None, f=None, x=None, y=None, k=None, a=None, tr=None,
                 p=None, before=None, turn_r=None):
        self.kind = kind
        self.role, self.source, self.src, self.which, self.branch, self.g = role, source, src, which, branch, g
        self.i, self.h, self.m, self.tt, self.of, self.col = i, h, m, tt, of, col
        self.kc, self.width, self.moving, self.n_tok, self.first, self.keys = kc, width, moving, n_tok, first, keys
        self.chunks, self.groups, self.items, self.parts, self.unit, self.wt = chunks, groups, items, parts, unit, wt
        self.u, self.evac, self.used, self.f, self.x, self.y = u, evac, used, f, x, y
        self.k, self.a, self.tr, self.p, self.before, self.turn_r, self.n = k, a, tr, p, before, turn_r, n


def order_of_work():
    steps = []
    n = dict(wt=0, u=0, tr=0, s=0, f=0, x=0, k=0, a=0, y=0, rel=0, p=0, stacked=0, b_items=0, ac_items=0, ups=0, counted=0)
    count = dict(act_pj=0, dve_pj=0, act_s=0, dve_s=0)
    pj_freed, s_freed = [], []
    last_out = None

    def take(name, k=1):
        n[name] += k
        return n[name] - k

    def freed(ring, engine, of):
        count[f"{engine}_{of}"] += 1
        ring.append((engine, count[f"{engine}_{of}"]))

    def unit(role, src, col, kc=KC, width=P, moving="h", n_tok=T, **more):
        st = Step("unit", role=role, src=src, col=col, kc=kc, width=width, moving=moving,
                  n_tok=n_tok, wt=take("wt"), u=take("u"), **more)
        freed(pj_freed, "act", "pj")
        st.evac = pj_freed[-1][1]
        if role in ("kv", "qi", "kiw", "q", "ak", "av", "mv"):
            st.f = take("f")
        if role in ("z", "mk", "cq", "gate"):
            st.x = take("x")
        if role == "up":
            st.x = n["x"] - 2
            take("u")
            freed(pj_freed, "act", "pj")
            st.n = take("ups")
        steps.append(st)
        return st

    def turned(specs, beside=()):
        units = []
        for k in range(len(specs) + 2):
            if k >= 2 and units[k - 2].role in ("kv", "qi", "kiw", "q", "ak"):
                steps.append(Step("halve", unit=units[k - 2], k=units[k - 2].k, before=n["stacked"]))
            if k < len(specs):
                role, src, col, more = specs[k]
                units.append(unit(role, src, col, **more))
            elif beside:
                role, src, col, more = beside[k - len(specs)]
                unit(role, src, col, **more)
            if k >= 2:
                st = units[k - 2]
                banks = {"kv": 2, "qi": 4, "kiw": 1, "q": 2, "ak": 4}.get(st.role, 0)
                if banks:
                    steps.append(Step("restack", unit=st, tr=take("tr", banks), k=st.k))
                    n["stacked"] = n["tr"]
            if 1 <= k <= len(specs):
                st = units[k - 1]
                if st.role not in ("av", "mv"):
                    st.k = take("k")
                steps.append(Step("turn", unit=st, tr=take("tr")))
                st.turn_r = steps[-1].tr

    def prepare(source, g):
        steps.append(Step("prepare", source=source, g=g, used=count["dve_pj"]))

    def finish(g):
        steps.append(Step("finish", g=g, tr=take("tr", 2 * NT), y=last_out.y, evac=last_out.evac))

    def norm(source, g):
        steps.append(Step("norm", source=source, g=g, tr=take("tr", KC)))

    def attention(branch, g):
        if branch == "b":
            items, keys = [(tt, h) for tt in range(NT) for h in range(8)], T * (g + 1)
        else:
            items, keys = [(None, h) for h in range(4 if branch == "c" else 8)], 256
        group = Step("attention", branch=branch, g=g, keys=keys, items=[])
        group.n = min(4, 3 * SEQ // keys) if branch == "b" else 2
        for tt, h in items:
            it = Step("item", tt=tt, h=h, a=take("a"), u=take("u"), chunks=[])
            it.i = len(group.items) % group.n
            it.keys, it.size = (admissible(g, tt), keys) if branch == "b" else (NT * 256, SEQ)
            freed(pj_freed, "dve", "pj")
            it.used = pj_freed[-1][1]
            it.n = take("b_items" if branch == "b" else "ac_items")
            for c, size in chunked(it.keys):
                it.chunks.append((c, size, take("s")))
                if branch == "b":
                    freed(s_freed, "dve", "s")
                else:
                    s_freed.append(("exp", it.a + 1))
            it.groups = -(-it.keys // T)
            it.tr, it.p = take("tr", it.groups), take("p", it.groups)
            group.items.append(it)
            it.parts = counted(g, PER_ITEM[g]) if branch != "b" else None
        group.x = n["x"]
        steps.append(group)

    def counted(g, k):
        first = n["counted"]
        n["counted"] = min(first + k, 32 * NT)
        return range(first, n["counted"])

    def select_bits(g, k):
        steps.append(Step("count", g=g, parts=counted(g, k)))

    def branch(which, g):
        steps.append(Step("split_y", y=take("y"), used=count["dve_pj"]))
        for m in range(0, KC, 2):
            for i in range(2):
                unit("gate", "w_in", GATES + which * D + (m + i) * P, m=m + i)
            unit("up", "w_branch", m * P, kc=BC, width=2 * P, moving="y", m=m, which=which, y=n["y"],
                 first=(which == 2), g=g)
            if which != 1:
                select_bits(g, PER_PAIR[g])
            elif m:
                steps.append(Step("split_m", g=g, m=m - 2, x=n["x"] - 2))
            if which != 1:
                pass
            elif m == 2 and g + 1 < NG:
                prepare("x", g + 1)
            elif m == 4 and g + 1 < NG:
                steps.append(Step("sines", g=g + 1))

    prepare("mem", 0)
    norm("mem", 0)
    for h in range(4):
        unit("mk", "w_mem_kv", h * P, n_tok=MEM, h=h)
    turned([("mv", "w_mem_kv", BW + h * P, dict(n_tok=MEM, h=h)) for h in range(4)])
    steps.append(Step("save_mem", x=n["x"], tr=n["tr"]))
    prepare("x", 0)
    steps.append(Step("sines", g=0))
    def gates_of(first, g):
        return [("z", "w_in", first + i * P, dict(i=i, g=g, y=n["y"])) for i in range(4)]

    for g in range(NG):
        n["counted"] = 0
        if g == 0:
            norm("x", g)
        turned([("kv", "w_in", B_KV, dict(g=g)),
                ("qi", "w_in", B_QI, dict(g=g, i=0)),
                ("qi", "w_in", B_QI + P, dict(g=g, i=1)),
                ("kiw", "w_in", B_KIW, dict(g=g, width=HD + 4))], beside=gates_of(C_Z, g)[:2])
        if g:
            finish(g - 1)
        st = Step("index", g=g, keys=T * (g + 1), parts=[], tr=n["tr"])
        for tt in range(NT):
            for h in range(4):
                for c, size in chunked(admissible(g, tt)):
                    st.parts.append((tt, h, c, size, take("s"), take("rel")))
                    freed(s_freed, "act", "s")
        steps.append(st)
        for role, src, col, more in gates_of(C_Z, g)[2:]:
            unit(role, src, col, **more)
            select_bits(g, PER_UNIT[g])
        for i in range(4):
            unit("cq", "w_in", C_Q + i * P, i=i)
            select_bits(g, PER_UNIT[g])
        attention("c", g)
        branch(2, g)
        for role, src, col, more in gates_of(A_Z, g)[:2]:
            unit(role, src, col, **more)
        select_bits(g, PER_UNIT[g])
        turned([("ak", "w_in", A_K, dict(g=g, y=n["y"])), ("av", "w_in", A_V, dict(g=g))]
               + [("q", "w_in", A_Q + i * P, dict(g=g, i=i)) for i in range(4)], beside=gates_of(A_Z, g)[2:])
        attention("a", g)
        branch(0, g)
        for role, src, col, more in gates_of(B_Z, g)[:2]:
            unit(role, src, col, **more)
        select_bits(g, 32 * NT)
        steps.append(Step("select", g=g, x=n["x"]))
        turned([("q", "w_in", B_Q + i * P, dict(g=g, i=i)) for i in range(4)], beside=gates_of(B_Z, g)[2:])
        attention("b", g)
        branch(1, g)
        steps.append(Step("load_rows", g=g, x=n["x"]))
        if g + 1 < NG:
            norm("x", g + 1)
        steps.append(Step("split_m", g=g, m=KC - 2, x=n["x"]))
        for m in range(KC):
            last_out = unit("out", "w_out", m * P, moving="m", m=m, g=g, y=n["y"])
    finish(NG - 1)
    return steps, pj_freed, s_freed, n


def hybrid_block(nc, x, mem, positions, g_in, w_in, attn_sinks, g_mem, w_mem_kv, w_branch, w_out,
                 g_final, out):
    steps, pj_freed, s_freed, _ = order_of_work()
    x_v = x[0].rearrange("(g t p) d -> g p t d", t=NT, p=P)
    out_v = out[0].rearrange("(g t p) d -> g p t d", t=NT, p=P)
    mem_v = mem[0].rearrange("(t p) d -> p t d", p=P)
    weights = {"w_in": w_in[0].rearrange("(k p) n -> p k n", p=P),
               "w_mem_kv": w_mem_kv[0].rearrange("(k p) n -> p k n", p=P),
               "w_out": w_out[0].rearrange("(k p) n -> p k n", p=P)}
    up_v = w_branch[0].rearrange("b (k p) n -> b p k n", p=P)
    mem_scratch = nc.dram_tensor("mem_scratch", (P, 4096), F32, kind="Internal").ap()

    ctx = ExitStack()
    with ctx:
        at = [(nc.sbuf_base + 63) // 64 * 64]

        def sb(name, shape, dt=F32, offset=None):
            size = int(np.prod(shape[1:])) * (1 if dt == mybir.dt.uint8 else 4)
            if offset is None:
                offset, at[0] = at[0], at[0] + (size + 31) // 32 * 32
            return nc.alloc_sbuf_tensor_at(name, shape, dt, offset=offset)

        def region(size):
            at[0] += size
            return at[0] - size

        def sem(name):
            return ctx.enter_context(nc.semaphore(name))

        hH, hL = sb("hH", [P, KC, T], F32R), sb("hL", [P, KC, T], F32R)
        raw, wH, wL = (sb(n, [P, 2, KC, P], d) for n, d in (("raw", F32), ("wH", F32R), ("wL", F32R)))
        kA, kB, kiS = (sb(n, [P, SEQ], F32R) for n in ("kA", "kB", "kiS"))
        vS = sb("vS", [P, SEQ // P, 3, HD], F32R)
        ckA, ckB, cv = (sb(n, [P, 2, P], F32R) for n in ("ckA", "ckB", "cv"))
        score_at = region(NT * SEQ * 4)
        score = sb("score", [P, NT, SEQ], offset=score_at)
        mergedL = sb("mergedL", [P, KC, T], F32R, offset=score_at)
        rows = sb("rows", [P, NT, D], offset=score_at + 2 * SEQ * 4)
        merged_at = region(16384)
        merged = sb("merged", [P, KC, T], offset=merged_at)
        ob = sb("ob", [P, KC, T], offset=merged_at)
        memkv = sb("memkv", [P, 4096], F32R, offset=merged_at)
        ys_at = region(16384)
        ysH, ysL = sb("ysH", [P, BC, T], F32R, ys_at), sb("ysL", [P, BC, T], F32R, ys_at + 8192)
        wkA, wkB = (sb(n, [P, 2, P + T], F32R, ys_at + o) for n, o in (("wkA", 0), ("wkB", 5120)))
        flags, ranks = sb("flags", [P, SEQ], F32, ys_at), sb("ranks", [P, SEQ], F32, ys_at + 8192)
        gfin = sb("gfin", [P, D], offset=ys_at)
        wv = sb("wv", [P, HD + (NT + 1) * 2 * P], F32R, ys_at + 10240)
        zs_at = region(8192)
        zs = sb("zs", [P, BC, T], offset=zs_at)
        qst_at = region(16384)
        qst = sb("qst", [P, 8, T], F32R, offset=qst_at)
        mergedH = sb("mergedH", [P, KC, T], F32R, offset=qst_at)
        p_at = region(3 * SEQ * 4)
        prob = sb("prob", [P, 3, SEQ], offset=p_at)
        xs = sb("xs", [P, NT, D], offset=p_at)
        squared = sb("squared", [P, D], offset=p_at + 16384)
        angles = sb("angles", [P, 4, NT, 32], offset=p_at + 20480)
        fT = sb("fT", [P, 2, T], offset=p_at)
        t1 = sb("t1", [P, T], offset=p_at + 4096)
        t2 = sb("t2", [P, T], offset=p_at + 6144)
        stack = sb("stack", [P, 2, 1024], F32R, offset=p_at + 8192)
        rel = sb("rel", [P, 2, 1024], offset=p_at + 8192)
        pt_at = region(8192)
        ptH = sb("ptH", [P, 2, T], F32R, offset=pt_at)
        ptL = sb("ptL", [P, 2, T], F32R, offset=pt_at + 4096)
        sg = sb("sg", [P, 2, T], offset=pt_at)
        ub = sb("ub", [P, 2, T], offset=pt_at + 4096)
        above_at = region(SEQ)
        above = sb("above", [P, SEQ], mybir.dt.uint8, offset=above_at)
        made = sb("made", [P, P], offset=above_at)
        rsum = sb("rsum", [P, 2 * P], offset=above_at + 512)
        cos, sin = sb("cos", [P, NT, 32]), sb("sin", [P, NT, 32])
        wmask = sb("wmask", [P, 2, 256], F32R)
        identR = sb("identR", [P, P], F32R)
        wi = sb("wi", [P, NT, 4])
        inv = sb("inv", [P, 32])
        posi, posf = sb("posi", [P, SEQ // P], I32), sb("posf", [P, SEQ // P])
        gcol = sb("gcol", [P, 2, KC])
        sink = sb("sink", [P, 8])
        small = sb("small", [P, 6, NT])
        ssq, var, rstd, tmp, cnt, need = (small[:, i, :] for i in range(6))
        rden, top, den = (sb(n, [P, 2, NT]) for n in ("rden", "top", "den"))
        snk, esnk, nmx, psum = (sb(n, [P, 2, NT]) for n in ("snk", "esnk", "nmx", "psum"))
        bits = sb("bits", [P, 5, NT], I32)
        ubits, cand, flip, thr, gi = (bits[:, i, :] for i in range(5))
        assert at[0] <= nc.sbuf_usable_end, at[0]
        ang, turns, *folded = (angles[:, i, :, :] for i in range(4))

        def t1_heads(nh):
            return t1[:, 0:NT * nh * HD].rearrange("p (n c) -> p n c", c=HD)

        def banked(bank, size):
            return bank[:, 0:size] if size <= 512 else bank[:, :].rearrange("p (a c) -> p a c", a=2)[:, :, 0:size // 2]

        def halved(chunk):
            size = chunk.shape[1]
            return chunk if size <= 512 else chunk.rearrange("p (a c) -> p a c", a=2)

        def held(it, branch):
            return prob[:, :, :].rearrange("p a c -> p (a c)")[:, it.i * it.size:it.i * it.size + it.keys]

        def width(it, j):
            return min(T, it.keys - j * T)

        def stack_view(which, nh):
            return stack[:, which, 0:NT * nh * P].rearrange("p (n a c) -> p n a c", a=2, c=HD)

        def twice(ap, n):
            return ap.unsqueeze(2).broadcast_to([P, n, 2, HD])

        def tabled(table, n):
            return table[:, :, :].unsqueeze(2).broadcast_to([P, NT, n, 32])
        mKH = memkv[:, 0:1024].rearrange("p (h m) -> p h m", h=4)
        mKL = memkv[:, 1024:2048].rearrange("p (h m) -> p h m", h=4)
        mVH = memkv[:, 2048:3072].rearrange("p (t n) -> p t n", t=2)
        mVL = memkv[:, 3072:4096].rearrange("p (t n) -> p t n", t=2)

        PJ = [ctx.enter_context(nc.psum_tensor(f"PJ{i}", [P, T], F32)) for i in range(2)]
        TR = [ctx.enter_context(nc.psum_tensor(f"TR{i}", [P, T], F32)) for i in range(2)]
        SC = [ctx.enter_context(nc.psum_tensor(f"SC{i}", [P, 1024], F32)) for i in range(2)]

        names = """x_in rows_in half_done pos_in small_in gfin_in raw_in0 raw_in1 mem_out mem_in store
            hi_ready lo_ready tile_done act_pj dve_pj y_done tr_full tr_free s_full act_s dve_s
            pv_done stack_hi stack_lo roped rel_used mixed y_hi y_lo m_hi m_lo p_sub p_exp p_ready p_ready_ac rden_ready
            pt_hi h_hi squared var_ready rooted scaled selected out_ready consts dve_step pool_step
            act_step tables_in sin_ready ang_ready""".split()
        S = {n: sem(n) for n in names}
        raw_in = [S["raw_in0"], S["raw_in1"]]
        block = ctx.enter_context(nc.Block())
        freed_by = {"exp_s": S["p_exp"], "act_pj": S["act_pj"], "dve_pj": S["dve_pj"], "act_s": S["act_s"], "dve_s": S["dve_s"]}

        units = [st for st in steps if st.kind == "unit"]

        def tile_of(ring, un):
            c = 2 * P if un.role == "up" else P
            flat = ring[:, un.wt % 2, :, :].rearrange("p k c -> p (k c)")
            return flat[:, 0:un.kc * c].rearrange("p (k c) -> p k c", c=c)[:, :, 0:un.width]
        norms = [st for st in steps if st.kind == "norm"]

        def wait_bank(eng, ring, index, of):
            if index >= 2:
                engine, value = ring[index - 2]
                eng.wait_ge(freed_by[f"{engine}_{of}"], value)

        @block.sync
        def _(sp):
            def load_tile(wt):
                if wt >= 2:
                    sp.wait_ge(S["lo_ready"], wt - 1)
                st = units[wt]
                src = up_v[st.which] if st.src == "w_branch" else weights[st.src]
                sp.dma_start(tile_of(raw, st), src[:, :, st.col:st.col + st.width]).then_inc(raw_in[wt % 2], 16)

            sp.dma_start(xs[:, 0:2, :], mem_v).then_inc(S["x_in"], 16)
            sp.dma_start(posi[:, :], positions).then_inc(S["small_in"], 16)
            sp.dma_start(gcol[:, 0, :], g_mem).then_inc(S["small_in"], 16)
            sp.dma_start(gcol[:, 1, :], g_in).then_inc(S["small_in"], 16)
            sp.dma_start(sink[:, :], attn_sinks.broadcast_to([P, 8])).then_inc(S["small_in"], 16)
            load_tile(0)
            load_tile(1)
            loads = 1
            for st in steps:
                if st.kind == "prepare" and st.source == "x":
                    if st.g:
                        sp.wait_ge(S["dve_pj"], st.used)
                    else:
                        sp.wait_ge(S["mem_out"], 16)
                    sp.dma_start(xs[:, :, :], x_v[st.g]).then_inc(S["x_in"], 16)
                elif st.kind == "save_mem":
                    sp.wait_ge(S["mixed"], st.x)
                    sp.wait_ge(S["tr_free"], st.tr)
                    sp.dma_start(mem_scratch, memkv[:, :].bitcast(F32)).then_inc(S["mem_out"], 16)
                elif st.kind == "unit":
                    if st.wt + 2 < len(units):
                        load_tile(st.wt + 2)
                elif st.kind == "load_rows":
                    sp.wait_ge(S["mixed"], st.x)
                    sp.dma_start(rows[:, :, :], x_v[st.g]).then_inc(S["rows_in"], 16)
                    sp.dma_start(gfin[:, :], g_final.unsqueeze(0).broadcast_to([P, D])).then_inc(S["gfin_in"], 16)
                elif st.kind == "finish":
                    sp.wait_ge(S["out_ready"], st.g + 1)
                    sp.dma_start(out_v[st.g], rows[:, :, :]).then_inc(S["store"], 16)
                    if st.g + 1 < NG:
                        sp.wait_ge(S["tr_free"], st.tr + 2 * NT)
                        sp.dma_start(memkv[:, :].bitcast(F32), mem_scratch).then_inc(S["mem_in"], 16)
            sp.wait_ge(S["store"], 16 * NG)

        @block.tensor
        def _(pe):
            def transposes(tr, blocks, parts=False):
                if tr >= 2:
                    pe.wait_ge(S["tr_free"], tr - 1)
                for at_col, src in blocks:
                    k, m = src.shape[0], src.shape[1]
                    bank = TR[tr % 2][0:m, at_col:at_col + k]
                    if parts:
                        last = nc.tensor.transpose(bank.bitcast(F32R), src, identR[0:k, 0:k])
                    else:
                        last = nc.tensor.transpose(bank, src, identR[0:k, 0:k].bitcast(F32))
                last.then_inc(S["tr_full"], 1)

            def scores(it, branch, g, chunks=(0, 1)):
                for c, size, s in [it.chunks[i] for i in chunks if i < len(it.chunks)]:
                    wait_bank(pe, s_freed, s, "s")
                    bank = SC[s % 2]
                    if branch == "b":
                        lhs = qst[:, it.h, it.tt * P:(it.tt + 1) * P]
                        n = size if size <= 512 else size // 2
                        for half in range(size // n):
                            to, keys = bank[:, half * 512:half * 512 + n], slice(c + half * n, c + half * n + n)
                            nc.tensor.matmul(to, lhs, kA[:, keys], start=True, stop=False)
                            last = nc.tensor.matmul(to, lhs, kB[:, keys], start=False, stop=True)
                    for tt in range(NT if branch != "b" else 0):
                        o = tt * 256
                        tok = slice(tt * P, (tt + 1) * P)
                        if branch == "a":
                            lhs, kv = qst[:, it.h, tok], it.h // 4
                            keys = slice(tt * P, tt * P + 256)
                            nc.tensor.matmul(bank[:, o:o + 256], identR[:, :], wmask[:, 0 if g == 0 and tt == 0 else 1, :],
                                             start=True, stop=False)
                            nc.tensor.matmul(bank[:, o:o + 256], lhs, wkA[:, kv, keys], start=False, stop=False)
                            last = nc.tensor.matmul(bank[:, o:o + 256], lhs, wkB[:, kv, keys], start=False, stop=True)
                        elif branch == "c":
                            qh, ql = qst[:, it.h, tok], qst[:, 4 + it.h, tok]
                            nc.tensor.matmul(bank[:, o:o + 256], qh, mKH[:, it.h, :], start=True, stop=False)
                            nc.tensor.matmul(bank[:, o:o + 256], qh, mKL[:, it.h, :], start=False, stop=False)
                            last = nc.tensor.matmul(bank[:, o:o + 256], ql, mKH[:, it.h, :], start=False, stop=True)
                    last.then_inc(S["s_full"], 1)

            def turned(it, branch, j):
                slot = held(it, branch)
                if j == 0:
                    if branch == "b":
                        pe.wait_ge(S["p_exp"], it.a + 1)
                    else:
                        pe.wait_ge(S["p_ready_ac"], it.n + 1)
                if branch == "b":
                    cols = [(4 * j + i) * P for i in range(width(it, j) // P)]
                else:
                    cols = [tt * 256 + j * P for tt in range(NT)]
                transposes(it.tr + j, [(i * P, slot[:, c:c + P]) for i, c in enumerate(cols)])

            def products(it, branch, j):
                if j == 0:
                    wait_bank(pe, pj_freed, it.u, "pj")
                pe.wait_ge(S["tr_free"], it.tr + j + 1)
                H, L = ptH[:, (it.p + j) % 2, :], ptL[:, (it.p + j) % 2, :]
                bank, odd = PJ[it.u % 2], it.h % 2
                end = j == it.groups - 1
                blocks = 1 if branch == "c" else width(it, j) // P
                for b in range(blocks):
                    p = slice(b * P, (b + 1) * P)
                    if branch == "c":
                        vh, vl = mVH[:, j, it.h * P:(it.h + 1) * P], mVL[:, j, it.h * P:(it.h + 1) * P]
                        col, p = slice(0, T), slice(0, T)
                    elif branch == "b":
                        v = vS[:, 4 * j + b, :, :].rearrange("p a c -> p (a c)")
                        vh, vl = v[:, 0:P], v[:, P:P + HD]
                        col = slice(0, P)
                    else:
                        base, col = ((b + j) * 2 + it.h // 4) * P, p
                        vh = wv[:, base:base + P] if odd else wv[:, HD + base:2 * HD + base]
                        vl = wv[:, HD + base:HD + base + P] if odd else wv[:, 2 * HD + base:3 * HD + base]
                    last_block = end and (branch != "b" or b == blocks - 1)
                    for i, (v, pr) in enumerate(((vh, H), (vl, H), (vh, L))):
                        m = HD if (branch == "a" and not odd) or (branch == "b" and i == 1) else P
                        last = nc.tensor.matmul(bank[0:m, col], v, pr[:, p], start=(j == 0 and b == 0 and i == 0),
                                                stop=(last_block and i == 2), skip_group_check=True)
                last.then_inc(S["pv_done"], 1)

            pe.wait_ge(S["consts"], 1)
            for st in steps:
                if st.kind == "norm":
                    nt = 2 if st.source == "mem" else NT
                    pe.wait_ge(S["scaled"], norms.index(st) + 1)
                    for k in range(KC):
                        transposes(st.tr + k, [(t * P, xs[:, t, k * P:(k + 1) * P]) for t in range(nt)])
                    pe.wait_ge(S["tr_free"], st.tr + KC)
                elif st.kind == "unit":
                    pe.wait_ge(S["lo_ready"], st.wt + 1)
                    if st.moving == "y":
                        pe.wait_ge(S["y_lo"], st.y)
                    mH, mL = {"y": (ysH, ysL), "m": (mergedH, mergedL), "h": (hH, hL)}[st.moving]
                    vH, vL = tile_of(wH, st), tile_of(wL, st)
                    halves = 2 if st.role == "up" else 1
                    for half in range(halves):
                        wait_bank(pe, pj_freed, st.u + half, "pj")
                        cols = slice(half * P, min((half + 1) * P, st.width))
                        o = PJ[(st.u + half) % 2][0:cols.stop - cols.start, 0:st.n_tok]
                        for k in range(st.kc):
                            if st.moving == "m" and st.m == 0:
                                pe.wait_ge(S["m_lo"], st.g * KC + k + 1)
                            for i, (lhs, rhs) in enumerate(((vH, mH), (vH, mL), (vL, mH))):
                                last = nc.tensor.matmul(o, lhs[:, k, cols], rhs[:, k, 0:st.n_tok],
                                                        start=(k == 0 and i == 0), stop=(k == st.kc - 1 and i == 2))
                        last.then_inc(S["tile_done" if half == halves - 1 else "half_done"], 1)
                elif st.kind == "turn":
                    un = st.unit
                    pe.wait_ge(S["act_pj"], un.evac)
                    src = fT[:, un.f % 2, :]
                    transposes(st.tr, [(t * P, src[0:un.width, t * P:(t + 1) * P]) for t in range(un.n_tok // P)])
                elif st.kind == "restack":
                    un = st.unit
                    pe.wait_ge(S["stack_lo"], st.k + 1)
                    nh = {"kv": 1, "kiw": 1}.get(un.role, 2)
                    for j in range({"kv": 2, "qi": 4, "kiw": 1, "q": 2, "ak": 4}[un.role]):
                        which, h = divmod(j, nh)
                        transposes(st.tr + j, [(t * P, stack[:, which, (t * nh + h) * P:(t * nh + h + 1) * P])
                                              for t in range(NT)], parts=True)
                elif st.kind == "index":
                    pe.wait_ge(S["tr_free"], st.tr)
                    for tt, h, c, size, s, _ in st.parts:
                        wait_bank(pe, s_freed, s, "s")
                        n = size if size <= 512 else size // 2
                        for half in range(size // n):
                            keys = slice(c + half * n, c + half * n + n)
                            for i in range(2):
                                last = nc.tensor.matmul(SC[s % 2][:, half * 512:half * 512 + n],
                                                        qst[:, 4 * i + h, tt * P:(tt + 1) * P], kiS[:, keys],
                                                        start=(i == 0), stop=(i == 1))
                        last.then_inc(S["s_full"], 1)
                elif st.kind == "attention":
                    if st.branch == "c":
                        pe.wait_ge(S["mixed"], st.x)
                        if st.g:
                            pe.wait_ge(S["mem_in"], 16 * st.g)
                    else:
                        pe.wait_ge(S["tr_free"], st.items[0].tr)
                    items, branch = st.items, st.branch
                    scores(items[0], branch, st.g)
                    scores(items[1], branch, st.g)
                    behind = None
                    for i, it in enumerate(items):
                        for j in range(it.groups):
                            turned(it, branch, j)
                            if behind:
                                products(behind[0], branch, behind[1])
                            behind = (it, j)
                            if i + 2 < len(items):
                                scores(items[i + 2], branch, st.g, [c for c in range(2) if min(2 * c, it.groups - 1) == j])
                    if behind:
                        products(behind[0], branch, behind[1])
                elif st.kind == "finish":
                    pe.wait_ge(S["act_pj"], st.evac)
                    for j in range(2 * NT):
                        tt, half = divmod(j, 2)
                        transposes(st.tr + j, [(m * P, ob[:, 4 * half + m, tt * P:(tt + 1) * P]) for m in range(4)])

        @block.scalar
        def _(act):
            def split_hi(wt):
                un = units[wt]
                act.wait_ge(raw_in[wt % 2], 16 * (wt // 2 + 1))
                if wt >= 2:
                    act.wait_ge(S["tile_done"], wt - 1)
                nc.scalar.activation(tile_of(wH, un), tile_of(raw, un), ACT.Copy).then_inc(S["hi_ready"], 1)

            n_squares = [0]

            def squares(tiles, src):
                for t in range(tiles):
                    if n_squares[0]:
                        act.wait_ge(S["squared"], n_squares[0])
                    n_squares[0] += 1
                    nc.scalar.activation(squared[:, :], src[:, t, :], ACT.Square,
                                         accum_out=ssq[:, t:t + 1]).then_inc(S["squared"], 1)

            def root(n, tiles):
                act.wait_ge(S["var_ready"], n)
                nc.scalar.activation(rstd[:, 0:tiles], var[:, 0:tiles], ACT.Sqrt).then_inc(S["rooted"], 1)

            def exps(it, branch, keys):
                act.wait_ge(S["p_sub"], it.a + 1)
                scale = (P if branch == "c" else HD) ** -0.5
                slot = held(it, branch)
                if branch == "b":
                    nc.scalar.activation(slot, slot, ACT.Exp, bias=nmx[:, it.a % 2, 0:1],
                                         scale=scale).then_inc(S["p_exp"], 1)
                else:
                    if branch == "a":
                        nc.scalar.activation(esnk[:, it.a % 2, :], snk[:, it.a % 2, :], ACT.Exp)
                    bank = SC[it.chunks[0][2] % 2]
                    for tt in range(NT):
                        cols = slice(tt * 256, tt * 256 + 256)
                        last = nc.scalar.activation(slot[:, cols], bank[:, cols], ACT.Exp, bias=nmx[:, it.a % 2, tt:tt + 1],
                                                    scale=scale, accum_out=psum[:, it.a % 2, tt:tt + 1])
                    last.then_inc(S["p_exp"], 1)

            def turned_hi(it, j):
                tr, p = it.tr + j, it.p + j
                act.wait_ge(S["tr_full"], tr + 1)
                if p >= 2:
                    act.wait_ge(S["pv_done"], p - 1)
                nc.scalar.activation(ptH[:, p % 2, 0:width(it, j)], TR[tr % 2][:, 0:width(it, j)], ACT.Copy).then_inc(S["pt_hi"], 1)

            turn_r = []
            n_prepared = n_root = 0
            split_hi(0)
            split_hi(1)
            for st in steps:
                if st.kind == "prepare":
                    n_prepared += 1
                    nt = 2 if st.source == "mem" else NT
                    if n_prepared == 1:
                        act.wait_ge(S["small_in"], 64)
                    act.wait_ge(S["x_in"], 16 * n_prepared)
                    squares(nt, xs)
                    n_root += 1
                    root(n_root, nt)
                elif st.kind == "sines":
                    for i, table in enumerate((sin, cos)):
                        act.wait_ge(S["ang_ready"], 2 * st.g + i + 1)
                        nc.scalar.activation(table[:, :, :], folded[i], ACT.Sin).then_inc(S["sin_ready"], 1)
                elif st.kind == "norm":
                    nt = 2 if st.source == "mem" else NT
                    for k in range(KC):
                        act.wait_ge(S["tr_full"], st.tr + k + 1)
                        nc.scalar.activation(hH[:, k, 0:nt * P], TR[(st.tr + k) % 2][:, 0:nt * P], ACT.Copy,
                                             scale=gcol[:, 0 if st.source == "mem" else 1, k:k + 1]).then_inc(S["h_hi"], 1)
                elif st.kind == "unit":
                    if st.role == "up":
                        act.wait_ge(S["half_done"], st.n + 1)
                        nc.scalar.activation(ub[:, st.x % 2, :], PJ[st.u % 2][:, :], ACT.Copy).then_inc(S["act_pj"], 1)
                    act.wait_ge(S["tile_done"], st.wt + 1)
                    if st.wt + 2 < len(units):
                        split_hi(st.wt + 2)
                    bank = PJ[st.u % 2][0:min(st.width, P), 0:st.n_tok]
                    if st.role in ("z", "mk", "cq", "gate") and st.x >= 2:
                        act.wait_ge(S["mixed"], st.x - 1)
                    if st.role in ("kv", "qi", "kiw", "q", "ak", "av", "mv"):
                        if st.f >= 2:
                            act.wait_ge(S["tr_full"], turn_r[st.f - 2] + 1)
                        nc.scalar.activation(fT[0:st.width, st.f % 2, 0:st.n_tok], bank, ACT.Copy).then_inc(S["act_pj"], 1)
                    elif st.role in ("mk", "cq"):
                        hi = mKH[:, st.h, :] if st.role == "mk" else qst[:, st.i, :]
                        nc.scalar.activation(hi, bank, ACT.Copy)
                        nc.scalar.activation(ub[:, st.x % 2, 0:st.n_tok], bank, ACT.Copy).then_inc(S["act_pj"], 1)
                    elif st.role == "z":
                        nc.scalar.activation(sg[:, st.x % 2, :], bank, ACT.Sigmoid)
                        nc.scalar.activation(ub[:, st.x % 2, :], bank, ACT.Copy).then_inc(S["act_pj"], 1)
                    elif st.role == "gate":
                        nc.scalar.activation(sg[:, st.x % 2, :], bank, ACT.Sigmoid).then_inc(S["act_pj"], 1)
                    elif st.role == "up":
                        nc.scalar.activation(ub[:, (st.x + 1) % 2, :], PJ[(st.u + 1) % 2][:, :], ACT.Copy).then_inc(S["act_pj"], 1)
                    elif st.role == "out":
                        nc.scalar.activation(ob[:, st.m, :], bank, ACT.Copy).then_inc(S["act_pj"], 1)
                elif st.kind == "turn":
                    turn_r.append(st.tr)
                elif st.kind == "halve":
                    un = st.unit
                    act.wait_ge(S["roped"], st.k + 1)
                    if st.k:
                        act.wait_ge(S["tr_full"], st.before)
                    nh = 1 if un.role in ("kv", "kiw") else 2
                    if un.role in ("q", "kiw"):
                        last = nc.scalar.activation(stack_view(0, nh)[:, :, 0, :], t1_heads(nh), ACT.Copy)
                    else:
                        last = nc.scalar.activation(stack_view(0, nh), twice(t1_heads(nh), NT * nh), ACT.Copy)
                    last.then_inc(S["stack_hi"], 1)
                elif st.kind == "index":
                    for tt, h, c, size, s, n in st.parts:
                        act.wait_ge(S["s_full"], s + 1)
                        if n >= 2:
                            act.wait_ge(S["rel_used"], n - 1)
                        nc.scalar.activation(halved(rel[:, n % 2, 0:size]), banked(SC[s % 2], size), ACT.Relu).then_inc(S["act_s"], 1)
                elif st.kind == "attention":
                    act.wait_ge(S["mixed"], st.x)
                    items, b = st.items, st.branch == "b"
                    ahead = 1 if b else 2
                    for it in items[:ahead]:
                        exps(it, st.branch, st.keys)
                    for i, it in enumerate(items):
                        for j in range(it.groups):
                            turned_hi(it, j)
                            if j == min(1, it.groups - 1) and i + ahead < len(items):
                                exps(items[i + ahead], st.branch, st.keys)
                elif st.kind == "split_y":
                    act.wait_ge(S["dve_pj"], st.used)
                    for k in range(BC):
                        nc.scalar.activation(ysH[:, k, :], zs[:, k, :], ACT.Copy).then_inc(S["y_hi"], 1)
                elif st.kind == "split_m":
                    act.wait_ge(S["mixed"], st.x)
                    for m in range(st.m, st.m + 2):
                        nc.scalar.activation(mergedH[:, m, :], merged[:, m, :], ACT.Copy).then_inc(S["m_hi"], 1)
                elif st.kind == "finish":
                    act.wait_ge(S["tr_free"], st.tr + 2 * NT)
                    squares(NT, rows)
                    n_root += 1
                    root(n_root, NT)

        @block.gpsimd
        def _(pool):
            done = [0]

            def link(ins):
                done[0] += 1
                ins.then_inc(S["pool_step"], 1)
                pool.wait_ge(S["pool_step"], done[0])

            def split_lo(wt):
                un = units[wt]
                pool.wait_ge(S["hi_ready"], wt + 1)
                nc.gpsimd.tensor_tensor(tile_of(wL, un), tile_of(raw, un), tile_of(wH, un).bitcast(F32), ALU.subtract).then_inc(S["lo_ready"], 1)

            link(nc.gpsimd.memset(made[:, :], 0.0))
            link(nc.gpsimd.affine_select(out=made[:, :], in_=made[:, :], compare_op=ALU.not_equal, fill=1.0,
                                         base=0, pattern=[[-1, P]], channel_multiplier=1))
            link(nc.gpsimd.tensor_copy(identR[:, :], made[:, :]))
            link(nc.gpsimd.memset(wmask[:, :, :].bitcast(F32), 0.0))
            link(nc.gpsimd.memset(wmask[0:64, 0, 0:128].bitcast(F32), MASKED))
            link(nc.gpsimd.memset(wmask[0:64, 1, 0:64].bitcast(F32), MASKED))
            link(nc.gpsimd.memset(wmask[0:64, :, 192:256].bitcast(F32), MASKED))
            link(nc.gpsimd.memset(wmask[64:128, :, 0:128].bitcast(F32), MASKED))
            freq = np.power(np.float32(THETA), -np.arange(32, dtype=np.float32) * 2 / HD).astype(np.float32)
            for j in range(32):
                link(nc.gpsimd.memset(inv[:, j:j + 1], float(freq[j])))
            link(nc.gpsimd.memset(vS[:, :, 1, :].bitcast(F32), 1.0))
            for carried in (ckA, ckB, cv):
                last = nc.gpsimd.memset(carried[:, :, :].bitcast(F32), 0.0)
            last.then_inc(S["consts"], 1)
            split_lo(0)
            split_lo(1)
            for st in steps:
                if st.kind == "unit":
                    if st.wt + 2 < len(units):
                        split_lo(st.wt + 2)
                    if st.role in ("mk", "cq", "z"):
                        pool.wait_ge(S["act_pj"], st.evac)
                        a, b = sg[:, st.x % 2, 0:st.n_tok], ub[:, st.x % 2, 0:st.n_tok]
                    if st.role == "mk":
                        nc.gpsimd.tensor_tensor(mKL[:, st.h, :], b, mKH[:, st.h, :].bitcast(F32), ALU.subtract).then_inc(S["mixed"], 1)
                    elif st.role == "cq":
                        nc.gpsimd.tensor_tensor(qst[:, 4 + st.i, :], b, qst[:, st.i, :].bitcast(F32), ALU.subtract).then_inc(S["mixed"], 1)
                    elif st.role == "z":
                        if st.y:
                            pool.wait_ge(S["y_lo"], st.y)
                        nc.gpsimd.tensor_tensor(zs[:, st.i, :], a, b, ALU.mult).then_inc(S["mixed"], 1)
                    elif st.role == "up":
                        for half in range(2):
                            pool.wait_ge(S["act_pj"], st.evac + half)
                            a, b = sg[:, (st.x + half) % 2, :], ub[:, (st.x + half) % 2, :]
                            sum_m = merged[:, st.m + half, :]
                            if st.first:
                                nc.gpsimd.tensor_tensor(sum_m, a, b, ALU.mult).then_inc(S["mixed"], 1)
                            else:
                                link(nc.gpsimd.tensor_tensor(b, a, b, ALU.mult))
                                nc.gpsimd.tensor_tensor(sum_m, sum_m, b, ALU.add).then_inc(S["mixed"], 1)
                elif st.kind == "halve":
                    un = st.unit
                    pool.wait_ge(S["stack_hi"], st.k + 1)
                    nh = 1 if un.role in ("kv", "kiw") else 2
                    hi = stack_view(0, nh).bitcast(F32)
                    if un.role in ("q", "kiw"):
                        last = nc.gpsimd.tensor_tensor(stack_view(0, nh)[:, :, 1, :], t1_heads(nh), hi[:, :, 0, :], ALU.subtract)
                    else:
                        last = nc.gpsimd.tensor_tensor(stack_view(1, nh), twice(t1_heads(nh), NT * nh), hi, ALU.subtract)
                    last.then_inc(S["stack_lo"], 1)
                elif st.kind == "attention" and st.branch != "b":
                    for it in st.items:
                        pool.wait_ge(S["rden_ready"], it.n + 1)
                        pr = held(it, st.branch).rearrange("p (t c) -> p t c", t=NT)
                        nc.gpsimd.tensor_tensor(pr, pr, rden[:, it.a % 2, :].unsqueeze(2).broadcast_to([P, NT, 256]),
                                                ALU.mult).then_inc(S["p_ready_ac"], 1)

        @block.vector
        def _(dve):
            done = [0]

            def link(ins):
                done[0] += 1
                ins.then_inc(S["dve_step"], 1)
                dve.wait_ge(S["dve_step"], done[0])

            TT, TS, STT = nc.vector.tensor_tensor, nc.vector.tensor_scalar, nc.vector.scalar_tensor_tensor
            n_root, n_squares = [0], [0]

            def inverse_rms(tiles):
                n_root[0] += 1
                n_squares[0] += tiles
                dve.wait_ge(S["squared"], n_squares[0])
                v, q, t = var[:, 0:tiles], rstd[:, 0:tiles], tmp[:, 0:tiles]
                TS(v, ssq[:, 0:tiles], 1.0 / D, EPS, ALU.mult, ALU.add).then_inc(S["var_ready"], 1)
                dve.wait_ge(S["rooted"], n_root[0])
                link(nc.vector.reciprocal(q, q))
                link(TT(t, q, q, ALU.mult))
                link(TT(t, t, v, ALU.mult))
                link(TS(t, t, -0.5, 1.5, ALU.mult, ALU.add))
                link(TT(q, q, t, ALU.mult))

            def cut(value, n_bits):
                m, e = np.frexp(value)
                return float(np.floor(m * 2 ** n_bits) / 2 ** n_bits * 2.0 ** e)

            def tables(g):
                full, parts = 2 * np.pi, []
                for n_bits in (8, 9, 9):
                    parts.append(cut(full, n_bits))
                    full -= parts[-1]
                parts.append(float(np.float32(full)))
                at_tok = posf[:, g * NT:(g + 1) * NT].unsqueeze(2).broadcast_to([P, NT, 32])
                link(TT(ang, at_tok, inv[:, :].unsqueeze(1).broadcast_to([P, NT, 32]), ALU.mult))
                magic = 1.5 * 2.0 ** 23
                for i in range(2):
                    link(TS(turns, ang, 0.5 / np.pi, 0.25 * i, ALU.mult, ALU.add))
                    link(TS(turns, turns, magic, -magic, ALU.add, ALU.add))
                    link(STT(folded[i], turns, -parts[0], ang, ALU.mult, ALU.add))
                    for c in parts[1:]:
                        link(STT(folded[i], turns, -c, folded[i], ALU.mult, ALU.add))
                    if i:
                        link(TS(folded[i], folded[i], np.pi / 2, None, ALU.add))
                    TS(folded[i], folded[i], 3.1415925, -3.1415925, ALU.min, ALU.max).then_inc(S["ang_ready"], 1)

            def rope(un, tr, k):
                bank = TR[tr % 2]
                dve.wait_ge(S["tr_full"], tr + 1)
                cols = bank[:, 0:NT * P].rearrange("p (t c) -> p t c", t=NT)
                nh = 1 if un.role in ("kv", "kiw") else 2
                if k:
                    dve.wait_ge(S["stack_hi"], k)
                    dve.wait_ge(S["stack_lo"], k)
                if un.role == "kv":
                    hi, lo = (vS[:, un.g * NT:(un.g + 1) * NT, part, :] for part in (0, 2))
                    link(nc.vector.tensor_copy(hi, cols[:, :, HD:P]))
                    TT(lo, cols[:, :, HD:P], hi.bitcast(F32), ALU.subtract)
                elif un.role == "kiw":
                    TS(wi[:, :, :], cols[:, :, HD:HD + 4], 2.0 ** -4, None, ALU.mult)
                n = 2 * nh
                src4 = cols[:, :, 0:nh * HD].rearrange("p t (n c) -> p t n c", c=32)
                t1v = t1[:, 0:NT * nh * HD].rearrange("p (t n c) -> p t n c", t=NT, c=32)
                t2v = t2[:, 0:NT * nh * HD].rearrange("p (t n c) -> p t n c", t=NT, c=32)
                TT(t1v, src4, tabled(cos, n), ALU.mult)
                for half in range(2):
                    step = TT(t2v[:, :, half::2, :], src4[:, :, 1 - half::2, :], tabled(sin, nh), ALU.mult)
                    if half:
                        step.then_inc(S["tr_free"], 1)
                dve.wait_ge(S["tr_free"], tr + 1)
                a, b = (t[:, 0:NT * nh * HD].rearrange("p (n a c) -> p n a c", a=2, c=32) for t in (t1, t2))
                TT(a[:, :, 0, :], a[:, :, 0, :], b[:, :, 0, :], ALU.subtract)
                TT(a[:, :, 1, :], a[:, :, 1, :], b[:, :, 1, :], ALU.add).then_inc(S["roped"], 1)

            def put(tr, dst):
                dve.wait_ge(S["tr_full"], tr + 1)
                nc.vector.tensor_copy(dst, TR[tr % 2][:, :]).then_inc(S["tr_free"], 1)

            def window_values(un, tr):
                dve.wait_ge(S["tr_full"], tr + 1)
                if un.role == "av":
                    dst = wv[:, HD + 2 * P:HD + 10 * P].rearrange("p (n c) -> p n c", c=P)
                    src = TR[tr % 2][:, :].rearrange("p (n c) -> p n c", c=HD)
                    hi, lo = dst[:, :, 0:HD], dst[:, :, HD:P]
                else:
                    src = TR[tr % 2][:, 0:MEM].rearrange("p (n c) -> p n c", c=P)
                    hi, lo = (m[:, :, un.h * P:(un.h + 1) * P] for m in (mVH, mVL))
                link(nc.vector.tensor_copy(hi, src))
                TT(lo, src, hi.bitcast(F32), ALU.subtract).then_inc(S["tr_free"], 1)

            def masked(it, i):
                a = it.a % 2
                c, size, s = it.chunks[i]
                dve.wait_ge(S["s_full"], s + 1)
                nc.vector.tensor_tensor_reduce(halved(held(it, "b")[:, c:c + size]), banked(SC[s % 2], size),
                                               halved(score[:, it.tt, c:c + size]), 1.0, LOWEST, ALU.add,
                                               ALU.max, top[:, a, i:i + 1]).then_inc(S["dve_s"], 1)
                if i + 1 == len(it.chunks):
                    dve.wait_ge(S["dve_s"], s_freed[s][1])
                    highest = top[:, a, 0:1]
                    if i:
                        link(TT(highest, highest, top[:, a, 1:2], ALU.max))
                    TS(nmx[:, a, 0:1], highest, -HD ** -0.5, None, ALU.mult).then_inc(S["p_sub"], 1)

            def maxima(it, branch):
                a, s = it.a % 2, it.chunks[0][2]
                dve.wait_ge(S["s_full"], s + 1)
                sc = SC[s % 2][:, :].rearrange("p (t c) -> p t c", t=NT)
                link(nc.vector.tensor_reduce(top[:, a, :], sc, AX.X, ALU.max))
                if branch == "a":
                    link(TS(top[:, a, :], top[:, a, :], HD ** -0.5, sink[:, it.h:it.h + 1], ALU.mult, ALU.max))
                    link(TS(nmx[:, a, :], top[:, a, :], -1.0, None, ALU.mult))
                    TS(snk[:, a, :], nmx[:, a, :], sink[:, it.h:it.h + 1], None, ALU.add).then_inc(S["p_sub"], 1)
                else:
                    TS(nmx[:, a, :], top[:, a, :], -P ** -0.5, None, ALU.mult).then_inc(S["p_sub"], 1)

            def reciprocals(it, branch):
                a = it.a % 2
                dve.wait_ge(S["p_exp"], it.a + 1)
                sums = psum[:, a, :]
                if branch == "a":
                    link(TT(den[:, a, :], sums, esnk[:, a, :], ALU.add))
                    sums = den[:, a, :]
                nc.vector.reciprocal(rden[:, a, :], sums).then_inc(S["rden_ready"], 1)

            def turned_lo(it, j):
                tr, p = it.tr + j, it.p + j
                dve.wait_ge(S["pt_hi"], p + 1)
                cols = slice(0, width(it, j))
                TT(ptL[:, p % 2, cols], TR[tr % 2][:, cols], ptH[:, p % 2, cols].bitcast(F32), ALU.subtract).then_inc(S["tr_free"], 1)

            def gated(it, branch):
                dve.wait_ge(S["pv_done"], it.p + it.groups)
                if branch == "c":
                    rows, tile, tok = slice(0, P), it.h, slice(0, T)
                else:
                    rows, tile = slice(HD * (it.h % 2), HD * (it.h % 2) + HD), it.h // 2
                    tok = slice(0, T) if it.tt is None else slice(it.tt * P, (it.tt + 1) * P)
                z = zs[rows, tile, tok]
                if branch == "b":
                    bank = PJ[it.u % 2]
                    link(nc.vector.reciprocal(rsum[0:HD, 0:P], bank[HD:P, 0:P]))
                    link(TT(rsum[rows, P:2 * P], bank[0:HD, 0:P], rsum[0:HD, 0:P], ALU.mult))
                    TT(z, z, rsum[rows, P:2 * P], ALU.mult).then_inc(S["dve_pj"], 1)
                    return
                TT(z, PJ[it.u % 2][rows, 0:tok.stop - tok.start], z, ALU.mult).then_inc(S["dve_pj"], 1)

            def as_float(bits_in):
                link(TS(flip, bits_in, 31, 0x7FFFFFFF, ALU.arith_shift_right, ALU.bitwise_xor))
                link(STT(thr, flip, -2 ** 31, bits_in, ALU.bitwise_or, ALU.bitwise_xor))

            def count(g, tt, compare):
                keys = admissible(g, tt)
                link(TS(above[:, 0:keys], score[:, tt, 0:keys], thr.bitcast(F32)[:, tt:tt + 1], 0.0, compare, ALU.add,
                        accum_out=cnt[:, tt:tt + 1]))

            def threshold(g, parts):
                for part in parts:
                    bit, tt = 31 - part // NT, part % NT
                    if tt == 0:
                        if bit == 31:
                            link(nc.vector.memset(ubits, 0))
                        link(TS(cand, ubits, 1 << bit if bit < 31 else -2 ** 31, None, ALU.bitwise_or))
                        as_float(cand)
                    count(g, tt, ALU.is_ge)
                    if tt == NT - 1:
                        link(TS(gi, cnt, TOPK - 0.5, None, ALU.is_ge))
                        link(STT(ubits, gi, bit, ubits, ALU.logical_shift_left, ALU.bitwise_or))

            def select(g, tt, phase):
                keys = admissible(g, tt)
                t, sc = thr.bitcast(F32)[:, tt:tt + 1], score[:, tt, 0:keys]
                fl, rk = flags[:, 0:keys], ranks[:, 0:keys]
                if phase == 0:
                    if tt == 0:
                        as_float(ubits)
                    count(g, tt, ALU.is_gt)
                    link(TS(need[:, tt:tt + 1], cnt[:, tt:tt + 1], -1.0, float(TOPK), ALU.mult, ALU.add))
                elif phase == 1:
                    link(TS(fl, sc, t, None, ALU.is_equal))
                elif phase == 2:
                    link(nc.vector.tensor_tensor_scan(rk, fl, fl, 0.0, ALU.add, ALU.max))
                elif phase == 3:
                    link(STT(fl, rk, need[:, tt:tt + 1], fl, ALU.is_le, ALU.mult))
                elif phase == 4:
                    link(STT(fl, sc, t, fl, ALU.is_gt, ALU.add))
                elif phase == 5:
                    link(TS(sc, fl, -1.0, -MASKED, ALU.add, ALU.mult))
                    link(bar(g, tt, MASKED))

            def bar(g, tt, value):
                keys = admissible(g, tt)
                for half in range(2):
                    first = g * T + tt * P + (half + 1) * CHUNK
                    if first < keys:
                        last = nc.vector.memset(score[half * 64:half * 64 + 64, tt, first:keys], value)
                return last

            dve.wait_ge(S["small_in"], 64)
            dve.wait_ge(S["consts"], 1)
            link(nc.vector.tensor_copy(posf[:, :], posi[:, :]))
            for st in steps:
                if st.kind == "prepare":
                    nt = 2 if st.source == "mem" else NT
                    inverse_rms(nt)
                    for t in range(nt):
                        last = TS(xs[:, t, :], xs[:, t, :], rstd[:, t:t + 1], None, ALU.mult)
                    last.then_inc(S["scaled"], 1)
                    if st.source == "x":
                        tables(st.g)
                elif st.kind == "norm":
                    n, nt = norms.index(st), 2 if st.source == "mem" else NT
                    for k in range(KC):
                        dve.wait_ge(S["h_hi"], n * KC + k + 1)
                        STT(hL[:, k, 0:nt * P], TR[(st.tr + k) % 2][:, 0:nt * P],
                            gcol[:, 0 if st.source == "mem" else 1, k:k + 1], hH[:, k, 0:nt * P].bitcast(F32),
                            ALU.mult, ALU.subtract).then_inc(S["tr_free"], 1)
                elif st.kind == "turn":
                    un = st.unit
                    if un.role == "kv":
                        dve.wait_ge(S["sin_ready"], 2 * un.g + 2)
                    if un.role == "ak":
                        dve.wait_ge(S["y_lo"], un.y)
                        dve.wait_ge(S["tr_full"], st.tr + 1)
                        nc.vector.tensor_copy(wkA[:, :, 0:P], ckA[:, :, :].bitcast(F32))
                        nc.vector.tensor_copy(wkB[:, :, 0:P], ckB[:, :, :].bitcast(F32))
                        nc.vector.tensor_copy(wv[:, HD:HD + 2 * P], cv[:, :, :].rearrange("p a c -> p (a c)").bitcast(F32))
                        nc.vector.memset(wv[:, 0:HD].bitcast(F32), 0.0)
                    if un.role in ("av", "mv"):
                        window_values(un, st.tr)
                    else:
                        rope(un, st.tr, un.k)
                elif st.kind == "restack":
                    un = st.unit
                    tok = slice(un.g * T, (un.g + 1) * T)
                    if un.role == "kv":
                        to = [kA[:, tok], kB[:, tok]]
                    elif un.role == "kiw":
                        to = [kiS[:, tok]]
                    elif un.role == "ak":
                        to = [wkA[:, 0, P:], wkA[:, 1, P:], wkB[:, 0, P:], wkB[:, 1, P:]]
                    elif un.role == "q":
                        to = [qst[:, 2 * un.i + h, :] for h in range(2)]
                    else:
                        to = [qst[:, 4 * i + 2 * un.i + h, :] for i in range(2) for h in range(2)]
                    for j, dst in enumerate(to):
                        put(st.tr + j, dst)
                elif st.kind == "index":
                    for tt, h, c, size, s, m in st.parts:
                        if st.g and (tt, h, c) == (1, 0, 0):
                            dve.wait_ge(S["store"], 16 * st.g)
                        dve.wait_ge(S["act_s"], s_freed[s][1])
                        sc, rl, wt = score[:, tt, c:c + size], rel[:, m % 2, 0:size], wi[:, tt, h:h + 1]
                        if h == 0:
                            ins = TS(sc, rl, wt, None, ALU.mult)
                        else:
                            ins = STT(sc, rl, wt, sc, ALU.mult, ALU.add)
                        ins.then_inc(S["rel_used"], 1)
                        dve.wait_ge(S["rel_used"], m + 1)
                        if h == 3 and c + size == admissible(st.g, tt):
                            link(bar(st.g, tt, LOWEST))
                elif st.kind == "count":
                    threshold(st.g, st.parts)
                elif st.kind == "select":
                    dve.wait_ge(S["mixed"], st.x)
                    for phase in range(6):
                        select(st.g, 0, phase)
                elif st.kind == "attention":
                    dve.wait_ge(S["mixed"], st.x)
                    items, branch = st.items, st.branch

                    def beside(it, j):
                        if branch != "b":
                            if j == 1:
                                threshold(st.g, it.parts)
                        elif j == 0 and it.tt + 1 < NT and it.h < 6:
                            if it.h == 0 and it.tt:
                                dve.wait_ge(S["dve_pj"], it.used - 1)
                            select(st.g, it.tt + 1, it.h)

                    def front(i, c):
                        if i < len(items) and c < len(items[i].chunks):
                            if branch == "b":
                                masked(items[i], c)
                            else:
                                maxima(items[i], branch)

                    for i in range(2):
                        front(i, 0)
                        front(i, 1)
                    if branch != "b":
                        reciprocals(items[0], branch)
                    for i, it in enumerate(items):
                        if branch != "b" and i + 1 < len(items):
                            reciprocals(items[i + 1], branch)
                        for j in range(it.groups):
                            turned_lo(it, j)
                            if j == 0 and i:
                                gated(items[i - 1], branch)
                            beside(it, j)
                            for c in range(2):
                                if min(2 * c + 1, it.groups - 1) == j:
                                    front(i + 2, c)
                    if branch == "a":
                        nc.vector.tensor_copy(ckA[:, :, :], wkA[:, :, T:T + P].bitcast(F32))
                        nc.vector.tensor_copy(ckB[:, :, :], wkB[:, :, T:T + P].bitcast(F32))
                        nc.vector.tensor_copy(cv[:, :, :].rearrange("p a c -> p (a c)"),
                                              wv[:, HD + NT * 2 * P:HD + (NT + 1) * 2 * P].bitcast(F32))
                    gated(items[-1], branch)
                elif st.kind == "split_y":
                    for k in range(BC):
                        dve.wait_ge(S["y_hi"], st.y * BC + k + 1)
                        last = TT(ysL[:, k, :], zs[:, k, :], ysH[:, k, :].bitcast(F32), ALU.subtract)
                    last.then_inc(S["y_lo"], 1)
                elif st.kind == "split_m":
                    for m in range(st.m, st.m + 2):
                        dve.wait_ge(S["m_hi"], st.g * KC + m + 1)
                        TT(mergedL[:, m, :], merged[:, m, :], mergedH[:, m, :].bitcast(F32), ALU.subtract).then_inc(S["m_lo"], 1)
                elif st.kind == "finish":
                    dve.wait_ge(S["rows_in"], 16 * (st.g + 1))
                    for j in range(2 * NT):
                        tt, half = divmod(j, 2)
                        dve.wait_ge(S["tr_full"], st.tr + j + 1)
                        row = rows[:, tt, half * T:(half + 1) * T]
                        TT(row, TR[(st.tr + j) % 2][:, :], row, ALU.add).then_inc(S["tr_free"], 1)
                    inverse_rms(NT)
                    dve.wait_ge(S["gfin_in"], 16 * (st.g + 1))
                    for t in range(NT):
                        last = STT(rows[:, t, :], rows[:, t, :], rstd[:, t:t + 1], gfin[:, :], ALU.mult, ALU.mult)
                    last.then_inc(S["out_ready"], 1)


_INS = ["x", "mem", "positions", "g_in", "w_in", "attn_sinks", "g_mem", "w_mem_kv", "w_branch", "w_out", "g_final"]


def kernel(**inputs):
    import concourse.bacc as bacc
    from concourse.bass_utils import run_bass_kernel_spmd

    nc = bacc.Bacc("TRN2", target_bir_lowering=False, num_devices=1, dynamic_dma_scratch_size=1024)
    arrays, args = {}, []
    for name in _INS:
        a = np.asarray(inputs[name])
        if name in ("positions", "g_in", "g_mem"):
            a = a.reshape(-1, P).T
        a = np.ascontiguousarray(a)
        arrays[f"in_{name}"] = a
        args.append(nc.dram_tensor(f"in_{name}", a.shape, mybir.dt.from_np(a.dtype), kind="ExternalInput").ap())
    out = nc.dram_tensor("out", (1, SEQ, D), F32, kind="ExternalOutput").ap()
    hybrid_block(nc, *args, out)
    result = run_bass_kernel_spmd(nc, [arrays], core_ids=[0])
    return result.results[0]["out"]
```
